# Optimizing a Trainium2 kernel written in Bass

```python
import math
import jax, jax.numpy as jnp
from jax import lax
import numpy as np

D_MODEL = 1024
BATCH = 1
SEQ = 256
DEPTH = 2

D_MIX = D_MODEL
GROUP_W = D_MIX // 4
MLA_HEADS = 4
MLA_NOPE = 64
MLA_ROPE = 32
MLA_V = GROUP_W // MLA_HEADS
MLA_Q_LORA = 192
MLA_KV_LORA = 128
ML_HEADS = 4
ML_DH = GROUP_W // ML_HEADS
ML_CHUNK = 64
SC_CH = GROUP_W
SC_WIDTH = 3
DF_HEADS = 4
DF_V = GROUP_W // DF_HEADS
DF_DK = DF_V // 2
Q_BLOCK = 128
ROPE_THETA = 10000.0
N_EXPERTS = 16
N_GROUPS = 4
E_PER_GROUP = N_EXPERTS // N_GROUPS
TOPK_GROUPS = 1
TOP_K = 2
D_EXPERT = 256
DN_ALPHA = (2 * DEPTH) ** 0.25
DN_BETA = (8 * DEPTH) ** -0.25
LN_EPS = 1e-5
RMS_EPS = 1e-6
IN_SIZES = (
    MLA_Q_LORA, MLA_KV_LORA, MLA_ROPE,
    GROUP_W, GROUP_W, GROUP_W, ML_HEADS, ML_HEADS, GROUP_W,
    SC_CH, SC_CH, SC_CH,
    2 * DF_HEADS * DF_DK, 2 * DF_HEADS * DF_DK, DF_HEADS * DF_V,
)
IN_COLS = sum(IN_SIZES)

kernel_name = "hybrid_mla_mlstm_conv_diffattn_grouped_moe"

def layer_norm(x):
    xf = x.astype(jnp.float32)
    mu = jnp.mean(xf, -1, keepdims=True)
    var = jnp.mean(jnp.square(xf - mu), -1, keepdims=True)
    return ((xf - mu) * lax.rsqrt(var + LN_EPS)).astype(x.dtype)

def rms_norm(x, g):
    xf = x.astype(jnp.float32)
    y = xf * lax.rsqrt(jnp.mean(xf * xf, -1, keepdims=True) + RMS_EPS)
    return y.astype(x.dtype) * g

def rope_tables(seq, dim):
    inv = 1.0 / (ROPE_THETA ** (jnp.arange(0, dim, 2, dtype=jnp.float32) / dim))
    ang = jnp.arange(seq, dtype=jnp.float32)[:, None] * inv[None, :]
    return jnp.cos(ang), jnp.sin(ang)

def apply_rope(x, cos, sin):
    x1, x2 = jnp.split(x, 2, axis=-1)
    cos = cos.astype(x.dtype)
    sin = sin.astype(x.dtype)
    return jnp.concatenate([x1 * cos - x2 * sin, x1 * sin + x2 * cos], axis=-1)

def split_cols(z):
    idx, acc = [], 0
    for sz in IN_SIZES[:-1]:
        acc += sz
        idx.append(acc)
    return jnp.split(z, idx, axis=-1)

def causal_block_attention(q, k, v, scale):
    b, g, s, dk = q.shape
    nb = s // Q_BLOCK
    qb = q.reshape(b, g, nb, Q_BLOCK, dk).transpose(2, 0, 1, 3, 4)
    key_pos = jnp.arange(s)

    def one_block(args):
        q_blk, start = args
        sc = jnp.einsum('bgqd,bgkd->bgqk', q_blk, k).astype(jnp.float32) * scale
        q_pos = start + jnp.arange(Q_BLOCK)
        sc = jnp.where(key_pos[None, :] <= q_pos[:, None], sc, -jnp.inf)
        p = jax.nn.softmax(sc, axis=-1).astype(v.dtype)
        return jnp.einsum('bgqk,bgkd->bgqd', p, v)

    out = lax.map(one_block, (qb, jnp.arange(nb) * Q_BLOCK))
    return out.transpose(1, 2, 0, 3, 4).reshape(b, g, s, v.shape[-1])

def mla_mixer(p_q, p_kv, k_rope, g_q, g_kv, w_uq, w_ukv, cos, sin):
    b, s, _ = p_q.shape
    q = (rms_norm(p_q, g_q) @ w_uq).reshape(b, s, MLA_HEADS, MLA_NOPE + MLA_ROPE).transpose(0, 2, 1, 3)
    kv = (rms_norm(p_kv, g_kv) @ w_ukv).reshape(b, s, MLA_HEADS, MLA_NOPE + MLA_V).transpose(0, 2, 1, 3)
    q_nope, q_pe = q[..., :MLA_NOPE], q[..., MLA_NOPE:]
    k_nope, v = kv[..., :MLA_NOPE], kv[..., MLA_NOPE:]
    q_pe = apply_rope(q_pe, cos, sin)
    k_pe = apply_rope(k_rope[:, None], cos, sin)
    qf = jnp.concatenate([q_nope, q_pe], -1)
    kf = jnp.concatenate([k_nope, jnp.broadcast_to(k_pe, k_nope.shape[:-1] + (MLA_ROPE,))], -1)
    o = causal_block_attention(qf, kf, v, (MLA_NOPE + MLA_ROPE) ** -0.5)
    return o.transpose(0, 2, 1, 3).reshape(b, s, MLA_HEADS * MLA_V)

def mlstm_mixer(q, k, v, i_pre, f_pre, o_pre):
    f32 = jnp.float32
    b, s, _ = q.shape
    L = ML_CHUNK
    nc = s // L

    def heads(t):
        return t.reshape(b, nc, L, ML_HEADS, ML_DH).transpose(0, 3, 1, 2, 4).astype(f32)

    def gates(t):
        return t.reshape(b, nc, L, ML_HEADS).transpose(0, 3, 1, 2).astype(f32)

    qh = heads(q) * (ML_DH ** -0.5)
    kh = heads(k)
    vh = heads(v)
    ig = gates(i_pre)
    lf = jax.nn.log_sigmoid(gates(f_pre))
    bcum = jnp.cumsum(lf, axis=-1)

    causal = jnp.tril(jnp.ones((L, L), dtype=bool))
    dmat = bcum[..., :, None] - bcum[..., None, :] + ig[..., None, :]
    dmat = jnp.where(causal, dmat, -jnp.inf)

    g_tot = bcum[..., -1]
    w_end = g_tot[..., None] - bcum + ig
    m_loc = jnp.max(w_end, axis=-1)
    a_end = jnp.exp(w_end - m_loc[..., None])
    c_loc = jnp.einsum('bhcl,bhcld,bhcle->bhcde', a_end, kh, vh)
    n_loc = jnp.einsum('bhcl,bhcld->bhcd', a_end, kh)

    def step(carry, inp):
        c_st, n_st, m_st = carry
        g, ml, cl, nl = inp
        m_new = jnp.maximum(g + m_st, ml)
        a = jnp.exp(g + m_st - m_new)
        bb = jnp.exp(ml - m_new)
        c_new = a[..., None, None] * c_st + bb[..., None, None] * cl
        n_new = a[..., None] * n_st + bb[..., None] * nl
        return (c_new, n_new, m_new), (c_st, n_st, m_st)

    init = (jnp.zeros((b, ML_HEADS, ML_DH, ML_DH), f32),
            jnp.zeros((b, ML_HEADS, ML_DH), f32),
            jnp.zeros((b, ML_HEADS), f32))
    xs = (jnp.moveaxis(g_tot, 2, 0), jnp.moveaxis(m_loc, 2, 0),
          jnp.moveaxis(c_loc, 2, 0), jnp.moveaxis(n_loc, 2, 0))
    _, (c_prev, n_prev, m_prev) = lax.scan(step, init, xs)
    c_prev = jnp.moveaxis(c_prev, 0, 2)
    n_prev = jnp.moveaxis(n_prev, 0, 2)
    m_prev = jnp.moveaxis(m_prev, 0, 2)

    inter_log = bcum + m_prev[..., None]
    m_j = jnp.maximum(inter_log, jnp.max(dmat, axis=-1))
    a_inter = jnp.exp(inter_log - m_j)
    a_intra = jnp.exp(dmat - m_j[..., None])
    s_qk = jnp.einsum('bhcjd,bhcsd->bhcjs', qh, kh) * a_intra
    num = (a_inter[..., None] * jnp.einsum('bhcjd,bhcde->bhcje', qh, c_prev)
           + jnp.einsum('bhcjs,bhcse->bhcje', s_qk, vh))
    den = a_inter * jnp.einsum('bhcjd,bhcd->bhcj', qh, n_prev) + jnp.sum(s_qk, axis=-1)
    h = num / jnp.maximum(jnp.abs(den), jnp.exp(-m_j))[..., None]
    h = h.transpose(0, 2, 3, 1, 4).reshape(b, s, ML_HEADS * ML_DH)
    return (jax.nn.sigmoid(o_pre.astype(f32)) * h).astype(q.dtype)

def short_conv_mixer(b_gate, c_gate, h, w_conv):
    u = c_gate * h
    y = lax.conv_general_dilated(u, w_conv[:, None, :], window_strides=(1,),
                                 padding=[(SC_WIDTH - 1, 0)],
                                 dimension_numbers=('NWC', 'WIO', 'NWC'),
                                 feature_group_count=SC_CH)
    return b_gate * y

def diff_attn_mixer(q, k, v, lq1, lk1, lq2, lk2, g_sub, lambda_init, cos, sin):
    b, s, _ = q.shape
    qh = q.reshape(b, s, 2 * DF_HEADS, DF_DK).transpose(0, 2, 1, 3)
    kh = k.reshape(b, s, 2 * DF_HEADS, DF_DK).transpose(0, 2, 1, 3)
    vh = v.reshape(b, s, DF_HEADS, DF_V).transpose(0, 2, 1, 3)
    qh = apply_rope(qh, cos, sin)
    kh = apply_rope(kh, cos, sin)
    v2 = jnp.repeat(vh, 2, axis=1)
    o = causal_block_attention(qh, kh, v2, DF_DK ** -0.5).reshape(b, DF_HEADS, 2, s, DF_V)
    lam = (jnp.exp(jnp.sum(lq1 * lk1).astype(jnp.float32))
           - jnp.exp(jnp.sum(lq2 * lk2).astype(jnp.float32)) + lambda_init)
    o = o[:, :, 0] - lam.astype(o.dtype) * o[:, :, 1]
    o = rms_norm(o, g_sub) * (1.0 - lambda_init)
    return o.transpose(0, 2, 1, 3).reshape(b, s, DF_HEADS * DF_V)

def grouped_moe(u, w_router, b_router, w1, w3, w2):
    b, s, d = u.shape
    t = u.reshape(b * s, d)
    scores = jax.nn.sigmoid((t @ w_router).astype(jnp.float32))
    sel = scores + b_router.astype(jnp.float32)
    grp_score = jnp.sum(lax.top_k(sel.reshape(-1, N_GROUPS, E_PER_GROUP), 2)[0], axis=-1)
    _, gidx = lax.top_k(grp_score, TOPK_GROUPS)
    gmask = jnp.any(gidx[..., None] == jnp.arange(N_GROUPS), axis=1)
    emask = jnp.repeat(gmask, E_PER_GROUP, axis=1)
    _, eidx = lax.top_k(jnp.where(emask, sel, -jnp.inf), TOP_K)
    w = jnp.take_along_axis(scores, eidx, axis=1)
    w = w / jnp.sum(w, axis=-1, keepdims=True)
    gates = jnp.sum(jax.nn.one_hot(eidx, N_EXPERTS, dtype=jnp.float32) * w[..., None], axis=1)
    h = jax.nn.silu(jnp.einsum('td,edf->tef', t, w1)) * jnp.einsum('td,edf->tef', t, w3)
    y = jnp.einsum('tef,efd->td', h * gates.astype(h.dtype)[..., None], w2)
    return y.reshape(b, s, d)

def setup_inputs(seed: int = 0) -> dict:
    key = jax.random.key(seed)
    ks = iter(jax.random.split(key, 32))
    f32 = jnp.float32
    L = DEPTH

    def nrm(shape, scale):
        return jax.random.normal(next(ks), shape, f32) * scale

    def gain(shape):
        return 1.0 + nrm(shape, 0.02)

    return {
        "x": nrm((BATCH, SEQ, D_MODEL), 1.0),
        "c": nrm((BATCH, D_MODEL), 1.0),
        "w_ada": nrm((L, D_MODEL, 6 * D_MODEL), 0.5 * D_MODEL ** -0.5),
        "b_ada": nrm((L, 6 * D_MODEL), 0.02),
        "w_in": nrm((L, D_MODEL, IN_COLS), D_MODEL ** -0.5),
        "mla_g_q": gain((L, MLA_Q_LORA)),
        "mla_g_kv": gain((L, MLA_KV_LORA)),
        "mla_w_uq": nrm((L, MLA_Q_LORA, MLA_HEADS * (MLA_NOPE + MLA_ROPE)), MLA_Q_LORA ** -0.5),
        "mla_w_ukv": nrm((L, MLA_KV_LORA, MLA_HEADS * (MLA_NOPE + MLA_V)), MLA_KV_LORA ** -0.5),
        "ml_b_i": nrm((L, ML_HEADS), 0.1),
        "ml_b_f": jnp.linspace(3.0, 6.0, ML_HEADS, dtype=f32)[None, :] + nrm((L, ML_HEADS), 0.1),
        "sc_w": nrm((L, SC_WIDTH, SC_CH), SC_WIDTH ** -0.5),
        "df_lq1": nrm((L, DF_DK), 0.1),
        "df_lk1": nrm((L, DF_DK), 0.1),
        "df_lq2": nrm((L, DF_DK), 0.1),
        "df_lk2": nrm((L, DF_DK), 0.1),
        "df_g": gain((L, DF_V)),
        "w_out": nrm((L, D_MIX, D_MODEL), DN_BETA * D_MIX ** -0.5),
        "ln1_g": gain((L, D_MODEL)),
        "ln1_b": nrm((L, D_MODEL), 0.02),
        "w_router": nrm((D_MODEL, N_EXPERTS), D_MODEL ** -0.5),
        "b_router": nrm((N_EXPERTS,), 0.01),
        "w1": nrm((L, N_EXPERTS, D_MODEL, D_EXPERT), D_MODEL ** -0.5),
        "w3": nrm((L, N_EXPERTS, D_MODEL, D_EXPERT), D_MODEL ** -0.5),
        "w2": nrm((L, N_EXPERTS, D_EXPERT, D_MODEL), DN_BETA * D_EXPERT ** -0.5),
        "ln2_g": gain((L, D_MODEL)),
        "ln2_b": nrm((L, D_MODEL), 0.02),
    }

def reference(x, c, w_ada, b_ada, w_in, mla_g_q, mla_g_kv, mla_w_uq, mla_w_ukv, ml_b_i, ml_b_f,
              sc_w, df_lq1, df_lk1, df_lq2, df_lk2, df_g, w_out, ln1_g, ln1_b,
              w_router, b_router, w1, w3, w2, ln2_g, ln2_b):
    s = x.shape[1]
    cos_a, sin_a = rope_tables(s, MLA_ROPE)
    cos_d, sin_d = rope_tables(s, DF_DK)
    c_act = jax.nn.silu(c)
    for l in range(DEPTH):
        mod = (c_act @ w_ada[l] + b_ada[l])[:, None, :]
        sh1, sc1, g1, sh2, sc2, g2 = jnp.split(mod, 6, axis=-1)

        u = layer_norm(x) * (1.0 + sc1) + sh1
        (a_q, a_kv, a_kr, m_q, m_k, m_v, m_i, m_f, m_o,
         c_b, c_c, c_h, d_q, d_k, d_v) = split_cols(u @ w_in[l])
        y_a = mla_mixer(a_q, a_kv, a_kr, mla_g_q[l], mla_g_kv[l], mla_w_uq[l], mla_w_ukv[l], cos_a, sin_a)
        y_b = mlstm_mixer(m_q, m_k, m_v, m_i + ml_b_i[l], m_f + ml_b_f[l], m_o)
        y_c = short_conv_mixer(c_b, c_c, c_h, sc_w[l])
        lambda_init = 0.8 - 0.6 * math.exp(-0.3 * l)
        y_d = diff_attn_mixer(d_q, d_k, d_v, df_lq1[l], df_lk1[l], df_lq2[l], df_lk2[l], df_g[l],
                              lambda_init, cos_d, sin_d)
        mix = jnp.concatenate([y_a, y_b, y_c, y_d], axis=-1) @ w_out[l]
        x = layer_norm(DN_ALPHA * x + g1 * mix) * ln1_g[l] + ln1_b[l]

        u2 = layer_norm(x) * (1.0 + sc2) + sh2
        ffn = grouped_moe(u2, w_router, b_router, w1[l], w3[l], w2[l])
        x = layer_norm(DN_ALPHA * x + g2 * ffn) * ln2_g[l] + ln2_b[l]
    return x


_drawn_inputs = setup_inputs


def setup_inputs(seed=0):
    import zlib

    import numpy as np

    out = dict(_drawn_inputs(seed))
    spreads = {}
    factors = {'mla_g_q': 8.0,
     'mla_g_kv': 8.0,
     'mla_w_uq': 2.813,
     'ml_b_i': 3.382,
     'df_lq1': 5.457,
     'df_lk1': 4.554,
     'df_lq2': 8.0,
     'df_lk2': 6.02,
     'df_g': 8.0}
    for name, (base, spread) in spreads.items():
        noise = np.random.default_rng([zlib.crc32(name.encode()), seed]).standard_normal(out[name].shape)
        drawn = base * np.exp(spread * noise) if base else spread * noise
        out[name] = __import__('jax').numpy.asarray(drawn.astype(out[name].dtype))
    for name, factor in factors.items():
        out[name] = (out[name] * factor).astype(out[name].dtype)
    return out
```

```python
import math
from contextlib import ExitStack

import concourse.bass as bass
import numpy as np
from concourse import mybir

F32 = mybir.dt.float32
BF16 = mybir.dt.bfloat16
ALU = mybir.AluOpType
ACT = mybir.ActivationFunctionType
AX = mybir.AxisListType

P = 128
D = 1024
S = 256
NT = S // P
KC = D // P
DEPTH = 2
Q_LORA, KV_LORA, ROPE, NOPE = 192, 128, 32, 64
QK = NOPE + ROPE
NH = 4
DV = 64
DK = 32
GW = 256
N_EXP, N_GRP = 16, 4
F_EXP = 256
ALPHA = (2 * DEPTH) ** 0.25
LN_EPS = 1e-5
RMS_EPS = 1e-6
NEG = -1e30

W_IN_TILES = [(0, 256, "a"), (256, 96, "a2"), (2152, 256, "dq"), (2408, 256, "dk"), (2664, 256, "dv"),
              (1120, 264, "gates_o"), (864, 256, "mv"), (352, 256, "mq"), (608, 256, "mk"),
              (1384, 256, "cb"), (1640, 256, "cc"), (1896, 256, "ch")]
NW_IN = len(W_IN_TILES)
W_WIDTH = 264
W_SLOTS = 4
W_OUT_TILES = 4
W_TILES = NW_IN + W_OUT_TILES
E_SLOTS = 6
ADA_W = 1024
ADA_SLOTS = 3
ADA_COLS = 6 * D
ADA_TILES = KC * ADA_COLS // ADA_W
ADA_FIRST = KC * 2 * D // ADA_W

C_GQ, C_GKV, C_DFG, C_L, C_BI, C_BF, C_SC = 0, 192, 320, 384, 512, 513, 514
N_CUR = 520
K_COS, K_SIN, K_PRIO, K_LI = 0, 2 * ROPE, 4 * ROPE, 4 * ROPE + N_EXP
N_CONST = K_LI + 2 * DEPTH


def lambda_init(l):
    return 0.8 - 0.6 * math.exp(-0.3 * l)


def shape_constants():
    inv = (1.0 / (np.float32(10000.0) ** (np.arange(0, ROPE, 2, dtype=np.float32) / np.float32(ROPE)))).astype(np.float32)
    ang = np.arange(S, dtype=np.float32)[:, None] * inv[None, :]
    cos, sin = np.cos(ang).astype(np.float32), np.sin(ang).astype(np.float32)
    c = np.zeros((P, N_CONST), np.float32)
    for t in range(NT):
        c[:, K_COS + t * ROPE:K_COS + (t + 1) * ROPE] = np.concatenate([cos, cos], 1)[t * P:(t + 1) * P]
        c[:, K_SIN + t * ROPE:K_SIN + (t + 1) * ROPE] = np.concatenate([-sin, sin], 1)[t * P:(t + 1) * P]
    c[:, K_PRIO:K_PRIO + N_EXP] = np.arange(N_EXP, 0, -1)
    for l in range(DEPTH):
        c[:, K_LI + l] = lambda_init(l)
        c[:, K_LI + DEPTH + l] = 1.0 - lambda_init(l)
    m = np.zeros((P, 2 * P), np.float32)
    m[:, 0:P] = np.eye(P)
    m[:, P:] = np.where(np.arange(P)[None, :] > np.arange(P)[:, None], np.float32(NEG), np.float32(0))
    sel = np.zeros((NH, NH, P), np.float32)
    for h in range(NH):
        sel[h, h] = 1.0
    return c, m, sel.reshape(NH, NH * P)


def build(nc, a, out):
    ctx = ExitStack()
    with ctx:
        def sb(name, shape, dt=F32):
            return ctx.enter_context(nc.sbuf_tensor(name, shape, dt))

        def sem(name):
            return ctx.enter_context(nc.semaphore(name))

        bank = [ctx.enter_context(nc.psum_tensor(f"bank{i}", [P, 512], F32)) for i in range(8)]
        w_ring = [sb(f"w_ring{i}", [P, KC, W_WIDTH]) for i in range(W_SLOTS)]
        e_ring = [sb(f"e_ring{i}", [P, 2048]) for i in range(E_SLOTS)]
        ada_ring = [sb(f"ada_ring{i}", [P, ADA_W]) for i in range(ADA_SLOTS)]
        mod_acc = sb("mod_acc", [P, ADA_COLS])
        x_sb = sb("x_sb", [P, NT, D])
        uT = sb("uT", [P, KC, S])
        ln_gb = sb("ln_gb", [P, 2, D])
        gate_row = sb("gate_row", [P, 2, D])
        cur = sb("cur", [P, N_CUR])
        const = sb("const", [P, N_CONST])
        ident_mask = sb("ident_mask", [P, 2 * P])
        im_bf = sb("im_bf", [P, 2 * P], BF16)
        zeros_bf = sb("zeros_bf", [P, 512], BF16)
        ones = sb("ones", [P, P])
        ones_s = sb("ones_s", [NH, S])
        head_sel = sb("head_sel", [NH, NH * P])
        w_rt = sb("w_rt", [P, KC, N_EXP])
        b_rt = sb("b_rt", [P, N_EXP])
        c_col = sb("c_col", [P, KC])
        mcol = sb("mcol", [P, 2, 2, KC])
        st = sb("st", [P, NT, 2, 6])
        mv = sb("mv", [P, NT, 2])
        var = sb("var", [P, 8])
        rstd = sb("rstd", [P, 8])
        neg_half = sb("neg_half", [P, 8])
        uq = sb("uq", [P, NH * QK])
        uq_b = sb("uq_b", [Q_LORA - P, NH * QK])
        ukv = sb("ukv", [P, NH * 2 * DV])
        zA = sb("zA", [P, NT, 352])
        zD = sb("zD", [P, NT, 768])
        zG = sb("zG", [P, NT, 8])
        sig_o = sb("sig_o", [P, NT, GW])
        m_v = sb("m_v", [P, NT, GW])
        mqT = sb("mqT", [P, 2, S])
        mkT = sb("mkT", [P, 2, S])
        conv = sb("conv", [P, 1540])
        cbT = sb("cbT", [P, 2, S])
        tmp = sb("tmp", [P, 2 * D])
        kvn = sb("kvn", [P, NT, NH * 2 * DV])
        qf = sb("qf", [P, NT, NH * QK])
        kf = sb("kf", [P, NT, NH * QK])
        dT = sb("dT", [P, 4, S])
        prob = sb("prob", [P, 3, 384])
        rows = sb("rows", [NH, 4, S])
        nr_em = sb("nr_em", [P, 2, NT, NH])
        nmax = sb("nmax", [P, 12, NT])
        ssum = sb("ssum", [P, 12, NT])
        den = sb("den", [P, NT, NH])
        rden = sb("rden", [P, NT, NH])
        lam = sb("lam", [P, 8])
        score = sb("score", [P, NT, N_EXP])
        gates = sb("gates", [P, NT, N_EXP])
        rt = sb("rt", [P, 256])

        ident = ident_mask[:, 0:P]
        ones_row = ones_s[:, :]
        ident_bf = im_bf[:, 0:P]
        mask_bf = im_bf[:, P:2 * P]
        ccT = conv[:, 0:512].rearrange("p (c s) -> p c s", c=2)
        chT = conv[:, 512:1024].rearrange("p (c s) -> p c s", c=2)
        cuT = conv[:, 1024:1540].rearrange("p (c s) -> p c s", c=2)
        yN = conv[:, 0:1536].rearrange("p (t n) -> p t n", t=NT)
        xn = tmp[:, :].rearrange("p (t n) -> p t n", t=NT)
        t1 = tmp[:, 0:D]
        t2 = tmp[:, D:2 * D]
        qfT = t1[0:QK, :].rearrange("p (h s) -> p h s", h=NH)
        kfT = t2[0:QK, :].rearrange("p (h s) -> p h s", h=NH)
        decay, probT = qf, kf
        conv_y = zA[:, :, :].rearrange("p t n -> p (t n)")[:, 0:512].rearrange("p (c s) -> p c s", c=2)
        pT0 = prob[:, :, :].rearrange("p a b -> p (a b)")[:, 0:512]
        pT1 = prob[:, :, :].rearrange("p a b -> p (a b)")[0:Q_LORA - P, 512:768]
        silu = zD[:, :, :].rearrange("p t n -> p (t n)")[:, 0:512].rearrange("p (s n) -> p s n", s=2)
        sgate = zD[:, :, :].rearrange("p t n -> p (t n)")[:, 512:1024].rearrange("p (s n) -> p s n", s=2)
        hT = dT[:, 0:2, :]
        gdiag = dT[:, 2:4, :]

        def pair_rows(ap, n):
            return ap.unsqueeze(2).to_broadcast([P, ap.shape[1], n])

        const_in = sem("const_in")
        x_in = sem("x_in")
        setup = sem("setup")
        im_ready = sem("im_ready")
        c_ready = sem("c_ready")
        acc_zero = sem("acc_zero")
        acc_bias = sem("acc_bias")
        w_in_sem = [sem(f"w_loaded{i}") for i in range(W_SLOTS)]
        w_free = sem("w_free")
        e_in_sem = [sem(f"e_loaded{i}") for i in range(E_SLOTS)]
        up_free = sem("up_free")
        down_free = sem("down_free")
        ada_in_sem = [sem(f"ada_loaded{i}") for i in range(ADA_SLOTS)]
        ada_free = sem("ada_free")
        small_in = sem("small_in")
        ln_in = sem("ln_in")
        layer_fin = sem("layer_fin")
        layer_go = sem("layer_go")
        tick = sem("tick")
        out_done = sem("out_done")

        layer_sems = []

        def lsem(name):
            s = sem(name)
            layer_sems.append(s)
            return s

        v = lsem("vector_chain")
        ac = lsem("scalar_chain")
        acc_first, acc_rest = lsem("acc_first"), lsem("acc_rest")
        mod_cols, mcol_ready = lsem("mod_cols"), lsem("mcol_ready")
        var_ready, rstd_ready, xn_ready = lsem("var_ready"), lsem("rstd_ready"), lsem("xn_ready")
        xt_done, ut_act, ut_dve = lsem("xt_done"), lsem("ut_act"), lsem("ut_dve")
        z_done, z_out = lsem("z_done"), lsem("z_out")
        lat_ready, lat_t, lat_act, lat_dve = lsem("lat_ready"), lsem("lat_t"), lsem("lat_act"), lsem("lat_dve")
        gate_t, gate_read = lsem("gate_t"), lsem("gate_read")
        f_ready, lf_ready, rows_ready, rows_t, rows_out = (lsem("f_ready"), lsem("lf_ready"), lsem("rows_ready"),
                                                           lsem("rows_t"), lsem("rows_out"))
        proj_done, q_out, kv_out = lsem("proj_done"), lsem("q_out"), lsem("kv_out")
        d_roped, d_t, d_out = lsem("d_roped"), lsem("d_t"), lsem("d_out")
        qk_ready, qk_t, qT_out, kT_out = lsem("qk_ready"), lsem("qk_t"), lsem("qT_out"), lsem("kT_out")
        lam_dots, lam_exp = lsem("lam_dots"), lsem("lam_exp")
        rows_g, rows_g_out, cols2 = lsem("rows_g"), lsem("rows_g_out"), lsem("cols2")
        s_done, max_ready, p_act, p_dve = lsem("s_done"), lsem("max_ready"), lsem("p_act"), lsem("p_dve")
        decay_ready, pt_done, pt_out, pv_done = lsem("decay_ready"), lsem("pt_done"), lsem("pt_out"), lsem("pv_done")
        o_read = lsem("o_read")
        y_ready, y_t, y_out_act, y_out_dve, conv_ready = (lsem("y_ready"), lsem("y_t"), lsem("y_out_act"),
                                                          lsem("y_out_dve"), lsem("conv_ready"))
        mix_done, ln1_used = lsem("mix_done"), lsem("ln1_used")
        logits, score_ready = lsem("logits"), lsem("score_ready")
        diag_ready, g_ready, h_done, silu_done, h_ready, y_step, sg_done = (
            lsem("diag_ready"), lsem("g_ready"), lsem("h_done"), lsem("silu_done"), lsem("h_ready"),
            lsem("y_step"), lsem("sg_done"))
        moe_done = lsem("moe_done")
        first_layer_sem = min(s.num for s in layer_sems)
        last_layer_sem = max(s.num for s in layer_sems)
        assert last_layer_sem - first_layer_sem + 1 == len(layer_sems)

        block = ctx.enter_context(nc.Block())

        NMAP = 16

        def end_of_layer(eng, l):
            eng.drain().then_inc(layer_fin, 1)
            eng.wait_ge(layer_go, l + 2)

        @block.sync
        def _(sp):
            sp.dma_start(c_col[:], a["c"].rearrange("b (p k) -> (b p) k", k=KC)).then_inc(const_in, 16)
            sp.dma_start(const[:], a["const"]).then_inc(const_in, 16)
            sp.dma_start(ident_mask[:], a["ident_mask"]).then_inc(const_in, 16)
            sp.dma_start(head_sel[:], a["head_sel"]).then_inc(const_in, 16)
            sp.dma_start(w_rt[:], a["w_router"].rearrange("(p k) n -> p k n", k=KC)).then_inc(const_in, 16)
            sp.dma_start(b_rt[:], a["b_router"].unsqueeze(0).to_broadcast([P, N_EXP])).then_inc(const_in, 16)
            sp.dma_start(x_sb[:], a["x"].rearrange("b (t p) d -> (b p) t d", p=P)).then_inc(x_in, 16)

            ada = a["w_ada"].rearrange("l (p k) n -> l k p n", k=KC)

            def load_ada(l, k, m, slot, nth):
                sp.wait_ge(ada_free, nth + 1)
                sp.dma_start(ada_ring[slot][:], ada[l, k, :, m * ADA_W:(m + 1) * ADA_W]).then_inc(ada_in_sem[slot], 16)

            for n in range(ADA_FIRST):
                load_ada(0, n // 2, n % 2, n % ADA_SLOTS, n)

            def load_w(l, n):
                sp.wait_ge(w_free, l * W_TILES + n + 1)
                if n < NW_IN:
                    c0, width, _ = W_IN_TILES[n]
                    src = a["w_in"].rearrange("l (p k) n -> l p k n", k=KC)[l, :, :, c0:c0 + width]
                else:
                    width = D // W_OUT_TILES
                    c0 = (n - NW_IN) * width
                    src = a["w_out"].rearrange("l (k p) n -> l p k n", p=P)[l, :, :, c0:c0 + width]
                sp.dma_start(w_ring[n % W_SLOTS][:, :, 0:width], src).then_inc(w_in_sem[n % W_SLOTS], 16)

            with sp.Fori(0, DEPTH) as l:
                for n in range(W_SLOTS):
                    load_w(l, n)
                with sp.If(l < 1):
                    for n in range(ADA_FIRST, ADA_TILES):
                        load_ada(0, (n - ADA_FIRST) // 4, 2 + (n - ADA_FIRST) % 4, n % ADA_SLOTS, n)
                for n in range(W_SLOTS, W_TILES):
                    load_w(l, n)
                with sp.Fori(0, N_EXP // 2) as i:
                    for j in range(2):
                        e = 2 * i + j
                        sp.wait_ge(up_free, l * N_EXP + e + 1)
                        for q, name in enumerate(("w1", "w3")):
                            sp.dma_start(e_ring[3 * j + q][:].rearrange("p (k f) -> p k f", k=KC),
                                         a[name].rearrange("l e (p k) f -> l e p k f", k=KC)[l, e]).then_inc(
                                e_in_sem[3 * j + q], 16)
                        sp.wait_ge(down_free, l * N_EXP + e + 1)
                        sp.dma_start(e_ring[3 * j + 2][:].rearrange("p (c n) -> p c n", c=2),
                                     a["w2"].rearrange("l e (c p) n -> l e p c n", p=P)[l, e]).then_inc(
                            e_in_sem[3 * j + 2], 16)
                    with sp.If(l < DEPTH - 1):
                        after = nc.s_assert_within(l + 1, 1, DEPTH - 1)
                        for m in range(ADA_COLS // ADA_W):
                            load_ada(after, i, m, m % ADA_SLOTS, (l + 1) * ADA_TILES + 6 * i + m)
            sp.wait_ge(out_done, 16)

        @block.gpsimd
        def _(pool):
            nc.gpsimd.memset(mod_acc[:], 0.0).then_inc(acc_zero, 1)
            nc.gpsimd.memset(ones[:], 1.0).then_inc(setup, 1)
            nc.gpsimd.memset(zeros_bf[:], 0.0).then_inc(setup, 1)
            nc.gpsimd.memset(ones_s[:], 1.0)
            nc.gpsimd.memset(neg_half[:], -0.5).then_inc(setup, 1)
            nc.gpsimd.sem_inc(layer_go, 1)
            pool.wait_ge(setup, 3)

            def root(n, width):
                pool.wait_ge(var_ready, n)
                nc.gpsimd.tensor_tensor(rstd[:, 0:width], var[:, 0:width], neg_half[:, 0:width],
                                        ALU.pow).then_inc(rstd_ready, 1)

            with pool.Fori(0, DEPTH) as l:
                root(1, 2)
                root(2, 4)
                root(3, 8)
                root(4, 2)
                root(5, 2)
                with pool.If(l < DEPTH - 1):
                    pool.wait_ge(cols2, 1)
                    nc.gpsimd.memset(mod_acc[:], 0.0).then_inc(acc_zero, 1)
                root(6, 2)
                pool.drain().then_inc(layer_fin, 1)
                pool.wait_ge(layer_fin, 4 * (l + 1))
                nc.gpsimd.sem_inc(tick, 1)
                nc.gpsimd.sem_clear(range(first_layer_sem, last_layer_sem + 1))
                nc.gpsimd.sem_inc(layer_go, 1)

        @block.scalar
        def _(act):
            act.wait_ge(acc_zero, 1)
            act.dma_start(mod_acc[0:1, :], a["b_ada"][0:1, :]).then_inc(acc_bias, 16)
            act.wait_ge(const_in, 16 * 6)
            nc.scalar.activation(c_col[:], c_col[:], ACT.Silu).then_inc(c_ready, 1)
            chain = [0]

            def evict_x(first_bank, cols):
                for k in range(KC // 2):
                    act.wait_ge(xt_done, xt_base[0] + 2 * (k // 2) + 2)
                    act.wait_ge(mcol_ready, cols + 1)
                    src = bank[first_bank + k // 2][:, (k % 2) * S:(k % 2 + 1) * S]
                    nc.scalar.activation(uT[:, k, :], src, ACT.Identity, bias=mcol[:, cols, 0, k:k + 1],
                                         scale=mcol[:, cols, 1, k:k + 1]).then_inc(ut_act, 1)

            xt_base = [0]
            with act.Fori(0, DEPTH) as l:
                def param(dst, src):
                    act.dma_start(dst, src).then_inc(small_in, 16)

                def row_param(c0, name, n):
                    param(cur[:, c0:c0 + n], a[name][bass.ds(l, 1), :].to_broadcast([P, n]))

                row_param(C_GQ, "mla_g_q", Q_LORA)
                row_param(C_GKV, "mla_g_kv", KV_LORA)
                row_param(C_DFG, "df_g", DV)
                for q, name in enumerate(("df_lq1", "df_lk1", "df_lq2", "df_lk2")):
                    row_param(C_L + q * DK, name, DK)
                with nc.allow_non_contiguous_dma(reason="a few words to a partition each"):
                    param(cur[0:NH, C_BI:C_BI + 1], a["ml_b_i"][bass.ds(l, 1), :].rearrange("a h -> h a"))
                    param(cur[0:NH, C_BF:C_BF + 1], a["ml_b_f"][bass.ds(l, 1), :].rearrange("a h -> h a"))
                    for c in range(2):
                        param(cur[:, C_SC + 3 * c:C_SC + 3 * c + 3],
                              a["sc_w"][bass.ds(l, 1), :, c * P:(c + 1) * P].rearrange("a w p -> (a p) w"))
                param(uq[:], a["mla_w_uq"][l, 0:P, :])
                param(uq_b[:], a["mla_w_uq"][l, P:Q_LORA, :])
                param(ukv[:], a["mla_w_ukv"][l])

                def ln_load(row, name):
                    act.dma_start(ln_gb[:, row, :], a[name][bass.ds(l, 1), :].to_broadcast([P, D])).then_inc(ln_in, 16)

                ln_load(0, "ln1_g")
                ln_load(1, "ln1_b")
                xt_base[0] = 0
                evict_x(0, 0)

                dest = {
                    "a": lambda t: (zA[:, t, 0:256], 1.0), "a2": lambda t: (zA[:, t, 256:352], 1.0),
                    "dq": lambda t: (zD[:, t, 0:256], DK ** -0.5), "dk": lambda t: (zD[:, t, 256:512], 1.0),
                    "dv": lambda t: (zD[:, t, 512:768], 1.0), "mv": lambda t: (m_v[:, t, :], 1.0),
                    "mq": lambda c: (mqT[:, c, :], DV ** -0.5), "mk": lambda c: (mkT[:, c, :], 1.0),
                    "cb": lambda c: (cbT[:, c, :], 1.0), "cc": lambda c: (ccT[:, c, :], 1.0),
                    "ch": lambda c: (chT[:, c, :], 1.0)}
                def latents_out():
                    act.wait_ge(lat_t, 1)
                    nc.scalar.activation(pT0, bank[0][:, :], ACT.Copy).then_inc(lat_act, 1)

                def log_gates():
                    act.wait_ge(f_ready, 1)
                    nc.scalar.activation(rows[:, 1, :], rows[:, 1, :], ACT.Exp).then_inc(ac, 1)
                    act.wait_ge(ac, 1)
                    nc.scalar.activation(rows[:, 1, :], rows[:, 1, :], ACT.Ln, bias=1.0).then_inc(lf_ready, 1)

                def queries_out():
                    for t in range(NT):
                        act.wait_ge(proj_done, t + 1)
                        nc.scalar.activation(qf[:, t, :], bank[3 if t == 0 else 1][:, 0:NH * QK], ACT.Copy,
                                             scale=QK ** -0.5).then_inc(q_out, 1)

                def d_out_all():
                    for t in range(NT):
                        act.wait_ge(d_t, t + 1)
                        nc.scalar.activation(dT[:, :, t * P:(t + 1) * P],
                                             bank[t][:, :].rearrange("p (b s) -> p b s", b=4), ACT.Copy).then_inc(d_out, 1)

                for n, (_, width, kind) in enumerate(W_IN_TILES):
                    for half in range(2):
                        step = 2 * n + half
                        src = bank[4 + step % 4]
                        act.wait_ge(z_done, step + 1)
                        if kind == "gates_o":
                            nc.scalar.activation(zG[:, half, :], src[:, 0:8], ACT.Copy)
                            nc.scalar.activation(sig_o[:, half, :], src[:, 8:264], ACT.Sigmoid).then_inc(z_out, 1)
                        else:
                            dst, scale = dest[kind](half)
                            nc.scalar.activation(dst, src[:, 0:width], ACT.Copy, scale=scale).then_inc(z_out, 1)
                    if n == 7:
                        latents_out()
                    if n == 8:
                        log_gates()
                    if n == 9:
                        queries_out()
                    if n == 11:
                        d_out_all()

                act.wait_ge(lam_dots, 1)
                nc.scalar.activation(lam[:, 2:4], lam[:, 0:2], ACT.Exp).then_inc(lam_exp, 1)
                act.wait_ge(rows_t, 1)
                nc.scalar.activation(nr_em[:, 1, :, :], bank[3][:, 8:16].rearrange("p (t h) -> p t h", t=NT), ACT.Exp,
                                     scale=-1.0)
                nc.scalar.activation(nr_em[:, 0, :, :], bank[3][:, 0:8].rearrange("p (t h) -> p t h", t=NT), ACT.Copy,
                                     scale=-1.0).then_inc(rows_out, 1)
                for t in range(NT):
                    act.wait_ge(qk_t, t + 1)
                    nc.scalar.activation(qfT[:, :, t * P:(t + 1) * P],
                                         bank[2 + t][0:QK, :].rearrange("p (h s) -> p h s", h=NH), ACT.Copy).then_inc(qT_out, 1)
                for g in range(2):
                    for half in range(2):
                        act.wait_ge(rows_g, 2 * g + half + 1)
                        nc.scalar.activation(gate_row[:, g, half * 512:(half + 1) * 512], bank[4 + 2 * g + half][:, :],
                                             ACT.Copy).then_inc(rows_g_out, 1)

                for m in range(NMAP):
                    act.wait_ge(s_done, m + 1)
                    if m < 12:
                        src = bank[m % 4]
                        act.wait_ge(max_ready, m + 1)
                        if m >= 3:
                            act.wait_ge(pt_done, m - 2)
                        nc.scalar.activation(prob[:, m % 3, 0:P], src[:, 0:P], ACT.Exp, bias=nmax[:, m, 0:1],
                                             accum_out=ssum[:, m, 0:1])
                        nc.scalar.activation(prob[:, m % 3, P:384], src[:, P:384], ACT.Exp, bias=nmax[:, m, 1:2],
                                             accum_out=ssum[:, m, 1:2]).then_inc(p_act, 1)
                    else:
                        h = m - 12
                        src = bank[2 * (h % 2)]
                        if h == 0:
                            act.wait_ge(rows_out, 1)
                        if h >= 2:
                            act.wait_ge(p_dve, h - 1)
                        nc.scalar.activation(decay[:, h % 2, 0:P], src[:, 0:P], ACT.Exp, bias=nr_em[:, 0, 0, h:h + 1])
                        nc.scalar.activation(decay[:, h % 2, P:384], src[:, P:384], ACT.Exp,
                                             bias=nr_em[:, 0, 1, h:h + 1]).then_inc(decay_ready, 1)

                for n, (b, c0) in enumerate(((4, 0), (5, 6), (6, 2))):
                    act.wait_ge(y_t, n + 1)
                    nc.scalar.activation(uT[:, c0:c0 + 2, :], bank[b][:, :].rearrange("p (c s) -> p c s", c=2),
                                         ACT.Copy).then_inc(y_out_act, 1)
                xt_base[0] = KC
                evict_x(4, 1)
                act.wait_ge(ln1_used, 1)
                ln_load(0, "ln2_g")
                ln_load(1, "ln2_b")
                act.wait_ge(logits, 1)
                nc.scalar.activation(score[:], bank[7][:, 0:NT * N_EXP].rearrange("p (t e) -> p t e", t=NT),
                                     ACT.Sigmoid).then_inc(score_ready, 1)
                with act.If(l < DEPTH - 1):
                    act.wait_ge(acc_zero, l + 2)
                    after = nc.s_assert_within(l + 1, 1, DEPTH - 1)
                    act.dma_start(mod_acc[0:1, :], a["b_ada"][bass.ds(after, 1), :]).then_inc(acc_bias, 16)
                with act.Fori(0, N_EXP // 2) as i:
                    for s in range(4):
                        act.wait_ge(h_done, 4 * i + s + 1)
                        act.wait_ge(h_ready, 4 * i + s + 1)
                        nc.scalar.activation(silu[:, s % 2, :], bank[4 + s % 2][:, 0:S], ACT.Silu).then_inc(silu_done, 1)
                end_of_layer(act, l)
            act.dma_start(out.rearrange("b (t p) d -> (b p) t d", p=P), x_sb[:]).then_inc(out_done, 16)
            act.wait_ge(out_done, 16)

        @block.vector
        def _(dve):
            nc.vector.sem_inc(ada_free, ADA_SLOTS)
            V = nc.vector
            chain = [0]

            def link(ins):
                chain[0] += 1
                ins.then_inc(v, 1)
                dve.wait_ge(v, chain[0])

            def ada_step(nth, slot, slot_round, k_col, m):
                dve.wait_ge(ada_in_sem[slot], 16 * slot_round)
                part = mod_acc[:, m * ADA_W:(m + 1) * ADA_W]
                V.scalar_tensor_tensor(out=part, in0=ada_ring[slot][:], scalar=k_col, in1=part,
                                       op0=ALU.mult, op1=ALU.add).then_inc(ada_free, 1)

            dve.wait_ge(c_ready, 1)
            dve.wait_ge(acc_bias, 16)
            V.tensor_copy(im_bf[:], ident_mask[:]).then_inc(im_ready, 1)
            for n in range(ADA_FIRST):
                if n >= 2:
                    dve.wait_ge(ada_free, ADA_SLOTS + n - 1)
                ada_step(n, n % ADA_SLOTS, n // ADA_SLOTS + 1, c_col[:, n // 2:n // 2 + 1], n % 2)
            dve.wait_ge(x_in, 16)

            def layer_stats(nth):
                for t in range(NT):
                    for half in range(2):
                        V.bn_stats(st[:, t, half, :], x_sb[:, t, half * 512:(half + 1) * 512]).then_inc(v, 1)
                        chain[0] += 1
                dve.wait_ge(v, chain[0])
                for t in range(NT):
                    V.bn_aggr(mv[:, t, :], st[:, t, :, :].rearrange("p a b -> p (a b)")).then_inc(v, 1)
                    chain[0] += 1
                dve.wait_ge(v, chain[0])
                V.tensor_scalar(var[:, 0:NT], mv[:, :, 1], LN_EPS, None, ALU.add).then_inc(var_ready, 1)
                dve.wait_ge(rstd_ready, nth)

            def normalise(t):
                return V.tensor_scalar(xn[:, t, :], x_sb[:, t, :], mv[:, t, 0:1], rstd[:, t:t + 1], ALU.subtract, ALU.mult)

            def evict_x(first_bank, cols, base):
                for k in range(KC // 2, KC):
                    dve.wait_ge(xt_done, base + 2 * (k // 2) + 2)
                    V.tensor_scalar(uT[:, k, :], bank[first_bank + k // 2][:, (k % 2) * S:(k % 2 + 1) * S],
                                    mcol[:, cols, 1, k:k + 1], mcol[:, cols, 0, k:k + 1], ALU.mult,
                                    ALU.add).then_inc(ut_dve, 1)

            def mod_columns(cols, b):
                V.tensor_copy(mcol[:, cols, 0, :], bank[b][:, 0:KC])
                V.tensor_scalar(mcol[:, cols, 1, :], bank[b][:, KC:2 * KC], 1.0, None, ALU.add).then_inc(mcol_ready, 1)
                dve.wait_ge(mcol_ready, cols + 1)

            def rotate(src, dst, heads, dst_heads=None):
                n = NT * heads * ROPE
                h = ROPE // 2

                def table(c0, lo, hi):
                    return const[:, c0:c0 + NT * ROPE].rearrange("p (t r) -> p t r", t=NT)[:, :, lo:hi].unsqueeze(2).to_broadcast(
                        [P, NT, heads, hi - lo])
                r1 = t1[:, 0:n].rearrange("p (t h r) -> p t h r", t=NT, h=heads)
                r2 = t2[:, 0:n].rearrange("p (t h r) -> p t h r", t=NT, h=heads)
                V.tensor_tensor(r1, src, table(K_COS, 0, ROPE), ALU.mult)
                V.tensor_tensor(r2[:, :, :, 0:h], src[:, :, :, h:ROPE], table(K_SIN, 0, h), ALU.mult)
                link(V.tensor_tensor(r2[:, :, :, h:ROPE], src[:, :, :, 0:h], table(K_SIN, h, ROPE), ALU.mult))
                if dst_heads:
                    r1 = r1.to_broadcast([P, NT, dst_heads, ROPE])
                    r2 = r2.to_broadcast([P, NT, dst_heads, ROPE])
                return V.tensor_tensor(dst, r1, r2, ALU.add)

            def residual(gate, banks_done, nth, ln_wait, l):
                for half in range(2):
                    for t in range(NT):
                        banks_done(t, half)
                        part = slice(half * 512, (half + 1) * 512)
                        w = tmp[:, (2 * half + t) * 512:(2 * half + t + 1) * 512]
                        link(V.tensor_tensor(w, bank[2 * t + half][:, :], gate_row[:, gate, part], ALU.mult))
                        link(V.scalar_tensor_tensor(out=x_sb[:, t, part], in0=x_sb[:, t, part], scalar=ALPHA, in1=w,
                                                    op0=ALU.mult, op1=ALU.add))
                layer_stats(nth)
                for t in range(NT):
                    link(normalise(t))
                ln_wait()
                for t in range(NT):
                    link(V.tensor_tensor(x_sb[:, t, :], xn[:, t, :], ln_gb[:, 0, :], ALU.mult))
                for t in range(NT):
                    last = V.tensor_tensor(x_sb[:, t, :], x_sb[:, t, :], ln_gb[:, 1, :], ALU.add)
                    if t == NT - 1:
                        return last
                    link(last)

            with dve.Fori(0, DEPTH) as l:
                chain[0] = 0
                dve.drain().then_inc(acc_first, 1)
                layer_stats(1)
                for t in range(NT):
                    normalise(t).then_inc(xn_ready, 1)
                dve.wait_ge(mod_cols, 1)
                mod_columns(0, 7)
                evict_x(0, 0, 0)
                with dve.If(l < 1):
                    for n in range(ADA_FIRST, ADA_TILES):
                        if n >= ADA_FIRST + 4:
                            dve.wait_ge(ada_free, ADA_SLOTS + n - 3)
                        q = n - ADA_FIRST
                        ada_step(n, n % ADA_SLOTS, n // ADA_SLOTS + 1, c_col[:, q // 4:q // 4 + 1], 2 + q % 4)
                dve.drain().then_inc(acc_rest, 1)

                dve.wait_ge(small_in, 16 * 14 * (l + 1))
                dve.wait_ge(z_out, 4)
                for t in range(NT):
                    for q, (c0, n) in enumerate(((0, Q_LORA), (Q_LORA, KV_LORA))):
                        z = zA[:, t, c0:c0 + n]
                        ins = V.tensor_tensor_reduce(out=t1[:, (2 * t + q) * 192:(2 * t + q) * 192 + n], in0=z, in1=z, scale=1.0 / n, scalar=RMS_EPS, op0=ALU.mult,
                                                     op1=ALU.add, accum_out=var[:, 2 * t + q:2 * t + q + 1])
                ins.then_inc(var_ready, 1)
                dve.wait_ge(var_ready, 2)
                rotate(zA[:, :, 320:352].unsqueeze(2), kf[:, :, :].rearrange("p t (h c) -> p t h c", h=NH)[:, :, :, NOPE:QK],
                       1, NH).then_inc(v, 1)
                chain[0] += 1
                dve.wait_ge(rstd_ready, 2)
                for t in range(NT):
                    for q, (c0, n, g) in enumerate(((0, Q_LORA, C_GQ), (Q_LORA, KV_LORA, C_GKV))):
                        z = zA[:, t, c0:c0 + n]
                        ins = V.scalar_tensor_tensor(out=z, in0=z, scalar=rstd[:, 2 * t + q:2 * t + q + 1],
                                                     in1=cur[:, g:g + n], op0=ALU.mult, op1=ALU.mult)
                ins.then_inc(lat_ready, 1)
                for q in range(2):
                    c0 = C_L + 2 * q * DK
                    ins = V.tensor_tensor_reduce(out=rt[:, q * DK:(q + 1) * DK], in0=cur[:, c0:c0 + DK], in1=cur[:, c0 + DK:c0 + 2 * DK],
                                                 scale=1.0, scalar=0.0, op0=ALU.mult, op1=ALU.add, accum_out=lam[:, q:q + 1])
                ins.then_inc(lam_dots, 1)
                dve.wait_ge(z_out, 8)
                dve.wait_ge(v, chain[0])
                qk = zD[:, :, 0:512].rearrange("p t (h r) -> p t h r", h=16)
                rotate(qk, qk, 16).then_inc(d_roped, 1)
                dve.wait_ge(lat_t, 2)
                V.tensor_copy(pT1, bank[1][0:Q_LORA - P, 0:S]).then_inc(lat_dve, 1)

                dve.wait_ge(gate_t, 1)
                link(V.tensor_scalar(rows[:, 0, :], bank[2][0:NH, S:2 * S], cur[0:NH, C_BF:C_BF + 1], None, ALU.add))
                link(V.tensor_scalar(rows[:, 1, :], rows[:, 0, :], -1.0, None, ALU.mult))
                V.tensor_tensor(rows[:, 1, :], rows[:, 0, :], rows[:, 1, :], ALU.min).then_inc(f_ready, 1)
                dve.wait_ge(lf_ready, 1)
                link(V.scalar_tensor_tensor(out=rows[:, 0, :], in0=rows[:, 0, :], scalar=0.0, in1=rows[:, 1, :],
                                            op0=ALU.min, op1=ALU.subtract))
                link(V.tensor_tensor_scan(rows[:, 2, :], ones_row, rows[:, 0, :], 0.0, ALU.mult, ALU.add))
                link(V.scalar_tensor_tensor(out=rows[:, 1, :], in0=bank[2][0:NH, 0:S], scalar=cur[0:NH, C_BI:C_BI + 1],
                                            in1=rows[:, 2, :], op0=ALU.add, op1=ALU.subtract))
                link(V.tensor_tensor_scan(rows[:, 3, :], ones_row, rows[:, 1, :], 0.0, ALU.mult, ALU.max))
                V.tensor_tensor(rows[:, 2, :], rows[:, 2, :], rows[:, 3, :], ALU.add).then_inc(rows_ready, 1)

                for t in range(NT):
                    dve.wait_ge(proj_done, 3 + t)
                    V.tensor_copy(kvn[:, t, :], bank[0 if t == 0 else 2][:, :]).then_inc(kv_out, 1)
                dve.wait_ge(kv_out, NT)
                for t in range(NT):
                    V.tensor_copy(kf[:, t, :].rearrange("p (h c) -> p h c", h=NH)[:, :, 0:NOPE],
                                  kvn[:, t, :].rearrange("p (h c) -> p h c", h=NH)[:, :, 0:NOPE])
                dve.wait_ge(q_out, NT)
                qpe = qf[:, :, :].rearrange("p t (h c) -> p t h c", h=NH)[:, :, :, NOPE:QK]
                dve.wait_ge(d_roped, 1)
                rotate(qpe, qpe, NH).then_inc(qk_ready, 1)

                dve.wait_ge(z_out, 24)
                dve.wait_ge(z_done, 24)
                V.memset(cuT[:, :, 0:2], 0.0)
                link(V.tensor_tensor(cuT[:, :, 2:S + 2], ccT, chT, ALU.mult))
                y = conv_y
                dve.wait_ge(qk_ready, 1)
                for tap in (2, 1, 0):
                    for c in range(2):
                        w = cur[:, C_SC + 3 * c + tap:C_SC + 3 * c + tap + 1]
                        src = cuT[:, c, tap:tap + S]
                        if tap == 2:
                            ins = V.tensor_scalar(y[:, c, :], src, w, None, ALU.mult)
                        else:
                            ins = V.scalar_tensor_tensor(out=y[:, c, :], in0=src, scalar=w, in1=y[:, c, :],
                                                         op0=ALU.mult, op1=ALU.add)
                        ins.then_inc(v, 1)
                        chain[0] += 1
                    dve.wait_ge(v, chain[0])
                V.tensor_tensor(uT[:, 4:6, :], y, cbT[:], ALU.mult).then_inc(conv_ready, 1)
                for t in range(NT):
                    dve.wait_ge(qk_t, 3 + t)
                    V.tensor_copy(kfT[:, :, t * P:(t + 1) * P],
                                  bank[t][0:QK, :].rearrange("p (h s) -> p h s", h=NH)).then_inc(kT_out, 1)
                dve.wait_ge(lam_exp, 1)
                link(V.tensor_tensor(lam[:, 4:5], lam[:, 3:4], lam[:, 2:3], ALU.subtract))
                link(V.tensor_scalar(lam[:, 5:6], const[:, bass.ds(l + K_LI, 1)], -1.0, None, ALU.mult))
                link(V.tensor_tensor(lam[:, 6:7], lam[:, 4:5], lam[:, 5:6], ALU.add))
                link(V.tensor_scalar(lam[:, 7:8], const[:, bass.ds(l + (K_LI + DEPTH), 1)], 1.0, None, ALU.mult))
                link(V.tensor_scalar(cur[:, C_DFG:C_DFG + DV], cur[:, C_DFG:C_DFG + DV], lam[:, 7:8], None, ALU.mult))
                dve.wait_ge(cols2, 1)
                mod_columns(1, 3)

                def latent_y():
                    dve.wait_ge(p_act, NH)
                    link(V.reciprocal(ssum[:, 0:NH, :], ssum[:, 0:NH, :]))
                    dve.wait_ge(pv_done, NH)
                    for t in range(NT):
                        ins = V.tensor_tensor(yN[:, t, 0:GW].rearrange("p (h d) -> p h d", h=NH),
                                              bank[6][:, t * GW:(t + 1) * GW].rearrange("p (h d) -> p h d", h=NH),
                                              pair_rows(ssum[:, 0:NH, t], DV), ALU.mult)
                    ins.then_inc(y_ready, 1)

                def diff_y():
                    r = ssum[:, 4:12, :]
                    dve.wait_ge(p_act, 12)
                    link(V.reciprocal(r, r))
                    odd = r.rearrange("p (h two) t -> p h two t", two=2)[:, :, 1, :]
                    link(V.tensor_scalar(odd, odd, lam[:, 6:7], None, ALU.mult))
                    dve.wait_ge(pv_done, 12)
                    o = [tmp[:, t * 512:(t + 1) * 512].rearrange("p (m d) -> p m d", m=8) for t in range(NT)]
                    for t in range(NT):
                        V.tensor_tensor(o[t], bank[7 - t][:, :].rearrange("p (m d) -> p m d", m=8),
                                        pair_rows(ssum[:, 4:12, t], DV), ALU.mult).then_inc(o_read, 1)
                    dve.wait_ge(o_read, 2)
                    od = tmp[:, 1024:1536].rearrange("p (g d) -> p g d", g=NT * NH)
                    for t in range(NT):
                        om = o[t].rearrange("p (h two) d -> p h two d", two=2)
                        link(V.tensor_tensor(od[:, t * NH:(t + 1) * NH, :], om[:, :, 0, :], om[:, :, 1, :], ALU.add))
                    sq = tmp[:, 1536:2048].rearrange("p (g d) -> p g d", g=NT * NH)
                    link(V.tensor_tensor(sq, od, od, ALU.mult))
                    link(V.tensor_reduce(rt[:, 0:8], sq, AX.X, ALU.add))
                    V.tensor_scalar(var[:, 0:8], rt[:, 0:8], 1.0 / DV, RMS_EPS, ALU.mult, ALU.add).then_inc(var_ready, 1)
                    dve.wait_ge(rstd_ready, 3)
                    link(V.tensor_tensor(od, od, pair_rows(rstd[:, 0:8], DV), ALU.mult))
                    V.tensor_tensor(yN[:, :, 512:768].rearrange("p t (h d) -> p t h d", h=NH),
                                    od.rearrange("p (t h) d -> p t h d", t=NT),
                                    cur[:, C_DFG:C_DFG + DV].unsqueeze(1).unsqueeze(1).to_broadcast([P, NT, NH, DV]),
                                    ALU.mult).then_inc(y_ready, 1)

                def mlstm_y():
                    link(V.tensor_scalar(rden[:], den[:], -1.0, None, ALU.mult))
                    link(V.tensor_tensor(rden[:], rden[:], den[:], ALU.max))
                    link(V.tensor_tensor(rden[:], rden[:], nr_em[:, 1, :, :], ALU.max))
                    link(V.reciprocal(rden[:], rden[:]))
                    dve.wait_ge(pv_done, NMAP)
                    for t in range(NT):
                        ins = V.tensor_tensor(t1[:, t * GW:(t + 1) * GW].rearrange("p (h d) -> p h d", h=NH),
                                              bank[7][:, t * GW:(t + 1) * GW].rearrange("p (h d) -> p h d", h=NH),
                                              pair_rows(rden[:, t, :], DV), ALU.mult)
                    link(ins)
                    V.tensor_tensor(yN[:, :, 256:512], t1[:, 0:512].rearrange("p (t n) -> p t n", t=NT), sig_o[:],
                                    ALU.mult).then_inc(y_ready, 1)

                for m in range(NMAP + 2):
                    if m < 12:
                        dve.wait_ge(s_done, m + 1)
                        V.tensor_reduce(nmax[:, m, 0:1], bank[m % 4][:, 0:P], AX.X, ALU.max, negate=True)
                        V.tensor_reduce(nmax[:, m, 1:2], bank[m % 4][:, P:384], AX.X, ALU.max, negate=True).then_inc(max_ready, 1)
                    elif m < NMAP:
                        h = m - 12
                        dve.wait_ge(s_done, m + 1)
                        dve.wait_ge(decay_ready, h + 1)
                        dve.wait_ge(pt_done, m - 2)
                        for t, (lo, hi) in enumerate(((0, P), (P, 384))):
                            ins = V.tensor_tensor_reduce(out=prob[:, m % 3, lo:hi], in0=bank[2 * (h % 2) + 1][:, lo:hi],
                                                         in1=decay[:, h % 2, lo:hi], scale=1.0, scalar=0.0, op0=ALU.mult,
                                                         op1=ALU.add, accum_out=den[:, t, h:h + 1])
                        ins.then_inc(p_dve, 1)
                    if m >= 2:
                        w = m - 2
                        dve.wait_ge(pt_done, w + 1)
                        if w >= 2:
                            dve.wait_ge(pv_done, w - 1)
                        V.tensor_copy(probT[:, w % 2, :], bank[4 + w % 2][:, 0:384]).then_inc(pt_out, 1)
                    if m == NH + 2:
                        latent_y()
                    if m == 12 + 2:
                        diff_y()
                dve.wait_ge(p_dve, NH)
                mlstm_y()

                def mix_wait(t, half):
                    dve.wait_ge(mix_done, 4 * half + 3 + t)

                residual(0, mix_wait, 4, lambda: dve.wait_ge(ln_in, 64 * l + 32), l).then_inc(ln1_used, 1)
                dve.wait_ge(ln1_used, 1)
                layer_stats(5)
                for t in range(NT):
                    normalise(t).then_inc(xn_ready, 1)
                evict_x(4, 1, KC)
                dve.wait_ge(ut_dve, KC)

                def r_(c0, n, **kw):
                    ap = rt[:, c0:c0 + n]
                    return ap.rearrange(kw["as_"], **{k: x for k, x in kw.items() if k != "as_"}) if kw else ap
                sel = rt[:, 0:32]
                selt = sel.rearrange("p (t e) -> p t e", t=NT)
                selg = sel.rearrange("p (g e) -> p g e", e=4)
                pair = rt[:, 32:80].rearrange("p (g e) -> p g e", e=6)
                gs, gm, ge = rt[:, 80:88], rt[:, 88:90], rt[:, 90:98]
                gst, get = gs.rearrange("p (t g) -> p t g", t=NT), ge.rearrange("p (t g) -> p t g", t=NT)
                ms = rt[:, 98:130]
                one = [rt[:, 130:162], rt[:, 162:194]]
                mx, q1 = rt[:, 194:196], rt[:, 196:198]
                ws, wsum = rt[:, 198:230], rt[:, 230:232]
                prio_g = const[:, K_PRIO + N_EXP - N_GRP:K_PRIO + N_EXP].unsqueeze(1).to_broadcast([P, NT, N_GRP])
                prio_e = const[:, K_PRIO:K_PRIO + N_EXP].unsqueeze(1).to_broadcast([P, NT, N_EXP])

                def te(ap):
                    return ap.rearrange("p (t e) -> p t e", t=NT)

                dve.wait_ge(score_ready, 1)
                link(V.tensor_tensor(selt, score[:], b_rt[:].unsqueeze(1).to_broadcast([P, NT, N_EXP]), ALU.add))
                V.tensor_tensor(pair[:, :, 0:3], selg[:, :, 0:3], selg[:, :, 1:4], ALU.add)
                V.tensor_tensor(pair[:, :, 3:5], selg[:, :, 0:2], selg[:, :, 2:4], ALU.add)
                link(V.tensor_tensor(pair[:, :, 5:6], selg[:, :, 0:1], selg[:, :, 3:4], ALU.add))
                link(V.tensor_reduce(gs, pair, AX.X, ALU.max))
                link(V.tensor_reduce(gm, gst, AX.X, ALU.max))
                link(V.tensor_tensor(get, gst, pair_rows(gm, N_GRP), ALU.is_equal))
                link(V.tensor_tensor(get, get, prio_g, ALU.mult))
                link(V.tensor_reduce(gm, get, AX.X, ALU.max))
                link(V.tensor_tensor(get, get, pair_rows(gm, N_GRP), ALU.is_equal))
                link(V.tensor_scalar(ge, ge, -NEG, NEG, ALU.mult, ALU.add))
                link(V.tensor_tensor(ms.rearrange("p (g e) -> p g e", e=4), selg, pair_rows(ge, 4), ALU.add))
                for r in range(2):
                    link(V.tensor_reduce(mx, te(ms), AX.X, ALU.max))
                    link(V.tensor_tensor(te(one[r]), te(ms), pair_rows(mx, N_EXP), ALU.is_equal))
                    link(V.tensor_tensor(te(one[r]), te(one[r]), prio_e, ALU.mult))
                    link(V.tensor_reduce(q1, te(one[r]), AX.X, ALU.max))
                    link(V.tensor_tensor(te(one[r]), te(one[r]), pair_rows(q1, N_EXP), ALU.is_equal))
                    if r == 0:
                        link(V.scalar_tensor_tensor(out=ms, in0=one[0], scalar=NEG, in1=ms, op0=ALU.mult, op1=ALU.add))
                link(V.tensor_tensor(one[0], one[0], one[1], ALU.add))
                link(V.tensor_tensor(te(ws), score[:], te(one[0]), ALU.mult))
                link(V.tensor_reduce(wsum, te(ws), AX.X, ALU.add))
                link(V.reciprocal(wsum, wsum))
                link(V.tensor_tensor(gates[:], te(ws), pair_rows(wsum, N_EXP), ALU.mult))

                nc.vector.sem_inc(h_ready, 2)
                with dve.If(l < DEPTH - 1):
                    dve.wait_ge(acc_bias, 16 * (l + 2))
                    nc.vector.sem_inc(tick, 1)
                with dve.Fori(0, N_EXP // 2) as i:
                    for j in range(2):
                        for t in range(NT):
                            ins = V.tensor_scalar(gdiag[:, j, t * P:(t + 1) * P], ident, gates[:, t, bass.ds(2 * i + j, 1)],
                                                  None, ALU.mult)
                        ins.then_inc(diag_ready, 1)
                        for c in range(2):
                            s = 2 * j + c
                            dve.wait_ge(silu_done, 4 * i + s + 1)
                            if c == 0:
                                dve.wait_ge(g_ready, 2 * i + j + 1)
                            V.tensor_tensor(sgate[:, c, :], silu[:, c, :], bank[6 + j][:, 0:S], ALU.mult).then_inc(sg_done, 1)
                            dve.wait_ge(sg_done, 4 * i + s + 1)
                            dve.wait_ge(y_step, 4 * i + s + 1)
                            V.tensor_tensor(hT[:, c, :], sgate[:, c, :], bank[4 + c][:, S:2 * S], ALU.mult).then_inc(h_ready, 1)
                    with dve.If(l < DEPTH - 1):
                        base = (l + 1) * ADA_TILES + 6 * i
                        for m in range(6):
                            dve.wait_ge(ada_free, base + (ADA_SLOTS + m - 5))
                            ada_step(None, m % ADA_SLOTS, (l + 1) * (ADA_TILES // ADA_SLOTS) + 2 * i + m // ADA_SLOTS + 1,
                                     c_col[:, bass.ds(i, 1)], m)
                residual(1, lambda t, half: dve.wait_ge(moe_done, 1), 6, lambda: dve.wait_ge(ln_in, 64 * l + 64), l).then_inc(v, 1)
                end_of_layer(dve, l)

        @block.tensor
        def _(pe):
            nc.tensor.sem_inc(w_free, W_SLOTS)
            nc.tensor.sem_inc(up_free, 2)
            nc.tensor.sem_inc(down_free, 2)
            pe.wait_ge(setup, 3)
            pe.wait_ge(im_ready, 1)
            pe.wait_ge(const_in, 16 * 6)

            owed = []

            def then_free(mm):
                if owed:
                    mm.then_inc(owed.pop(), 1)
                return mm

            def mod_col(b, section, j):
                for k in range(KC):
                    cols = mod_acc[:, section * D + k:section * D + k + KC * (P - 1) + 1:KC]
                    mm = pe.matmul(bank[b][:, j * KC + k:j * KC + k + 1], cols, ones[:, 0:1], start=True, stop=True)
                return mm

            def turn_x(first_bank, base):
                for t in range(NT):
                    pe.wait_ge(xn_ready, base + t + 1)
                    for k in range(KC):
                        if k == 1 and t == 0:
                            then_free(mm)
                        mm = pe.transpose(bank[first_bank + k // 2][:, (k % 2) * S + t * P:(k % 2) * S + (t + 1) * P],
                                          xn[:, t, k:k + KC * (P - 1) + 1:KC], ident)
                        if t == NT - 1:
                            mm.then_inc(xt_done, 1)

            def w_step(l, n, half):
                kind, width = W_IN_TILES[n][2], W_IN_TILES[n][1]
                step = 2 * n + half
                w = w_ring[n % W_SLOTS]
                dst = bank[4 + step % 4]
                if half == 0:
                    pe.wait_ge(w_in_sem[n % W_SLOTS], 16 * (l * (W_TILES // W_SLOTS) + n // W_SLOTS + 1))
                if step >= 4:
                    pe.wait_ge(z_out, step - 3)
                for k in range(KC):
                    if k == 1:
                        then_free(mm)
                    if step == 0:
                        pe.wait_ge(ut_act if k < KC // 2 else ut_dve, k % (KC // 2) + 1)
                    if kind in ("mq", "mk", "cb", "cc", "ch"):
                        mm = pe.matmul(dst[:, 0:S], w[:, k, half * P:(half + 1) * P], uT[:, k, :], start=(k == 0), stop=(k == KC - 1))
                    else:
                        mm = pe.matmul(dst[:, 0:width], uT[:, k, half * P:(half + 1) * P], w[:, k, 0:width],
                                       start=(k == 0), stop=(k == KC - 1))
                mm.then_inc(z_done, 1)
                if half == 1:
                    owed.append(w_free)

            def turn_latents():
                pe.wait_ge(lat_ready, 1)
                for t in range(NT):
                    then_free(pe.transpose(bank[0][:, t * P:(t + 1) * P], zA[:, t, 0:P], ident))
                    mm = pe.transpose(bank[0][:, S + t * P:S + (t + 1) * P], zA[:, t, Q_LORA:Q_LORA + KV_LORA], ident)
                mm.then_inc(lat_t, 1)
                for t in range(NT):
                    mm = pe.transpose(bank[1][0:Q_LORA - P, t * P:(t + 1) * P], zA[:, t, P:Q_LORA], ident)
                mm.then_inc(lat_t, 1)

            def turn_gates():
                pe.wait_ge(z_out, 12)
                for q in range(2):
                    for t in range(NT):
                        mm = pe.transpose(bank[2][0:NH, q * S + t * P:q * S + (t + 1) * P], zG[:, t, q * NH:(q + 1) * NH], ident)
                mm.then_inc(gate_t, 1)

            def project_latents():
                pe.wait_ge(lat_act, 1)
                pe.wait_ge(lat_dve, 1)
                for t in range(NT):
                    dst = bank[3 if t == 0 else 1][:, 0:NH * QK]
                    then_free(pe.matmul(dst, pT0[:, t * P:(t + 1) * P], uq[:], start=True, stop=False))
                    pe.matmul(dst, pT1[:, t * P:(t + 1) * P], uq_b[:], start=False, stop=True).then_inc(proj_done, 1)
                for t in range(NT):
                    if t == 1:
                        pe.wait_ge(rows_ready, 1)
                    pe.matmul(bank[0 if t == 0 else 2][:, :], pT0[:, S + t * P:S + (t + 1) * P], ukv[:], start=True,
                              stop=True).then_inc(proj_done, 1)

            def turn_diff():
                pe.wait_ge(d_roped, 1)
                for t in range(NT):
                    if t == 0:
                        pe.wait_ge(kv_out, 1)
                    else:
                        pe.wait_ge(q_out, 2)
                    for b in range(4):
                        if b == 1:
                            then_free(mm)
                        mm = pe.transpose(bank[t][:, b * P:(b + 1) * P], zD[:, t, b * P:(b + 1) * P], ident)
                    mm.then_inc(d_t, 1)

            def turn_rows():
                pe.wait_ge(q_out, 1)
                for q, row in enumerate((3, 2)):
                    for t in range(NT):
                        mm = pe.transpose(bank[3][:, q * 8 + t * NH:q * 8 + (t + 1) * NH], rows[:, row, t * P:(t + 1) * P],
                                          ident[0:NH, 0:NH])
                mm.then_inc(rows_t, 1)

            def turn_qk():
                pe.wait_ge(qk_ready, 1)
                pe.wait_ge(kv_out, 2)
                pe.wait_ge(rows_out, 1)
                pe.wait_ge(d_out, 2)
                for q, src in enumerate((qf, kf)):
                    for t in range(NT):
                        dst = bank[2 + t if q == 0 else t]
                        for h in range(NH):
                            mm = pe.transpose(dst[0:QK, h * P:(h + 1) * P], src[:, t, h * QK:(h + 1) * QK], ident)
                        mm.then_inc(qk_t, 1)

            def gate_rows():
                pe.wait_ge(acc_rest, 1)
                for g, section in enumerate((2, 5)):
                    for half in range(2):
                        pe.wait_ge(z_out, 24)
                        c0 = section * D + half * 512
                        pe.matmul(bank[4 + 2 * g + half][:, :], ones[:], mod_acc[:, c0:c0 + 512], start=True,
                                  stop=True).then_inc(rows_g, 1)
                pe.wait_ge(qT_out, 2)
                mod_col(3, 3, 0)
                mod_col(3, 4, 1).then_inc(cols2, 1)

            def scores(m):
                if m < 4:
                    q, k = qfT[:, m, :], kfT[:, m, :]
                    dst = bank[m % 4]
                    if m == 0:
                        pe.wait_ge(qT_out, 2)
                        pe.wait_ge(kT_out, 2)
                    if m == 3:
                        pe.wait_ge(mcol_ready, 2)
                elif m < 12:
                    j = m - 4
                    r = slice(DK * (j % 4), DK * (j % 4) + DK)
                    q, k = dT[r, j // 4, :], dT[r, 2 + j // 4, :]
                    dst = bank[j % 4]
                    pe.wait_ge(p_act, m - 3)
                else:
                    h = m - 12
                    r = slice(DV * (h % 2), DV * (h % 2) + DV)
                    q, k = mqT[r, h // 2, :], mkT[r, h // 2, :]
                    dst = bank[2 * (h % 2) + 1]
                    if h < 2:
                        pe.wait_ge(p_act, 10 + 2 * h)
                    else:
                        pe.wait_ge(p_dve, h - 1)
                    log_decay = bank[2 * (h % 2)]
                    sel = head_sel[:, h * P:(h + 1) * P]
                    pe.matmul(log_decay[:, 0:P], sel, rows[:, 1, 0:P], start=True, stop=False)
                    pe.matmul(log_decay[:, 0:P], ident_bf, mask_bf, start=False, stop=True)
                    pe.matmul(log_decay[:, P:384], sel, rows[:, 1, :], start=True, stop=False)
                    pe.matmul(log_decay[:, 256:384], ident_bf, mask_bf, start=False, stop=True)
                    pe.matmul(dst[:, 0:P], q[:, 0:P], k[:, 0:P], start=True, stop=True)
                    return pe.matmul(dst[:, P:384], q[:, P:S], k, start=True, stop=True)
                pe.matmul(dst[:, 0:P], q[:, 0:P], k[:, 0:P], start=True, stop=False)
                pe.matmul(dst[:, 0:P], ident_bf, mask_bf, start=False, stop=True)
                pe.matmul(dst[:, P:384], q[:, P:S], k, start=True, stop=False)
                return pe.matmul(dst[:, 256:384], ident_bf, mask_bf, start=False, stop=True)

            def turn_probs(m):
                pe.wait_ge(p_act if m < 12 else p_dve, m + 1 if m < 12 else m - 11)
                if m >= 2:
                    pe.wait_ge(pt_out, m - 1)
                if m < 2:
                    pe.wait_ge(rows_g_out, 2)
                for b in range(3):
                    mm = pe.transpose(bank[4 + m % 2][:, b * P:(b + 1) * P], prob[:, m % 3, b * P:(b + 1) * P], ident)
                mm.then_inc(pt_done, 1)

            def values(m):
                pe.wait_ge(pt_out, m + 1)
                pT = probT[:, m % 2, :]
                if m < 4:
                    v_ = [kvn[:, t, m * 2 * DV + DV:(m + 1) * 2 * DV] for t in range(NT)]
                    dst = [bank[6][:, t * GW + m * DV:t * GW + (m + 1) * DV] for t in range(NT)]
                    if m == 0:
                        pe.wait_ge(rows_g_out, 4)
                elif m < 12:
                    j = m - 4
                    v_ = [zD[:, t, 512 + (j // 2) * DV:512 + (j // 2 + 1) * DV] for t in range(NT)]
                    dst = [bank[7 - t][:, j * DV:(j + 1) * DV] for t in range(NT)]
                    if m == 4:
                        pe.wait_ge(y_ready, 1)
                else:
                    h = m - 12
                    v_ = [m_v[:, t, h * DV:(h + 1) * DV] for t in range(NT)]
                    dst = [bank[7][:, t * GW + h * DV:t * GW + (h + 1) * DV] for t in range(NT)]
                    if h == 0:
                        pe.wait_ge(o_read, 2)
                pe.matmul(dst[0], pT[:, 0:P], v_[0], start=True, stop=True)
                pe.matmul(dst[1], pT[:, P:S], v_[0], start=True, stop=False)
                pe.matmul(dst[1], pT[:, S:384], v_[1], start=False, stop=True).then_inc(pv_done, 1)

            def turn_y(n):
                c0 = (0, 512, 256)[n]
                pe.wait_ge(y_ready, n + 1)
                if n == 0:
                    pe.wait_ge(pt_out, NMAP)
                for c in range(2):
                    for t in range(NT):
                        mm = pe.transpose(bank[4 + n][:, c * S + t * P:c * S + (t + 1) * P],
                                          yN[:, t, c0 + c * P:c0 + (c + 1) * P], ident)
                mm.then_inc(y_t, 1)

            def w_out_step(l, s):
                n = NW_IN + s
                w = w_ring[n % W_SLOTS]
                pe.wait_ge(w_in_sem[n % W_SLOTS], 16 * (l * (W_TILES // W_SLOTS) + n // W_SLOTS + 1))
                if s == 0:
                    pe.wait_ge(conv_ready, 1)
                    pe.wait_ge(y_out_act, 3)
                    pe.wait_ge(p_act, 12)
                    pe.wait_ge(p_dve, NH)
                for t in range(NT):
                    dst = bank[2 * t + s // 2][:, (s % 2) * 256:(s % 2 + 1) * 256]
                    for k in range(KC):
                        if k == 1:
                            then_free(mm)
                        mm = pe.matmul(dst, uT[:, k, t * P:(t + 1) * P], w[:, k, 0:256], start=(k == 0), stop=(k == KC - 1))
                    mm.then_inc(mix_done, 1)
                owed.append(w_free)

            def router():
                for t in range(NT):
                    for k in range(KC):
                        if t == 0:
                            pe.wait_ge(ut_act if k < KC // 2 else ut_dve, KC // 2 + k % (KC // 2) + 1)
                        if t == 0 and k == 0:
                            pe.wait_ge(ut_dve, KC)
                        mm = pe.matmul(bank[7][:, t * N_EXP:(t + 1) * N_EXP], uT[:, k, t * P:(t + 1) * P], w_rt[:, k, :],
                                       start=(k == 0), stop=(k == KC - 1))
                mm.then_inc(logits, 1)

            def expert_up(l, i, s):
                j, c = s // 2, s % 2
                if c == 0:
                    for q in range(2):
                        pe.wait_ge(e_in_sem[3 * j + q], 16 * (l * (N_EXP // 2) + i + 1))
                pe.wait_ge(h_ready, 4 * i + s + 1)
                for q in range(2):
                    w = e_ring[3 * j + q][:].rearrange("p (k f) -> p k f", k=KC)
                    for k in range(KC):
                        mm = pe.matmul(bank[4 + c][:, q * S:(q + 1) * S], w[:, k, c * P:(c + 1) * P], uT[:, k, :],
                                       start=(k == 0), stop=(k == KC - 1))
                        if q == 0 and k == 0:
                            mm.then_inc(y_step, 1)
                mm.then_inc(h_done, 1)

            def expert_gate(i, j):
                pe.wait_ge(diag_ready, 2 * i + j + 1)
                pe.matmul(bank[6 + j][:, 0:S], ones[:], gdiag[:, j, :], start=True, stop=True).then_inc(g_ready, 1)

            def expert_down(l, i, s):
                j, c = s // 2, s % 2
                if c == 0:
                    pe.wait_ge(e_in_sem[3 * j + 2], 16 * (l * (N_EXP // 2) + i + 1))
                pe.wait_ge(h_ready, 4 * i + s + 3)
                w = e_ring[3 * j + 2][:].rearrange("p (c n) -> p c n", c=2)
                for t in range(NT):
                    for half in range(2):
                        mm = pe.matmul(bank[2 * t + half][:, :], hT[:, c, t * P:(t + 1) * P],
                                       w[:, c, half * 512:(half + 1) * 512], start=False, stop=False, skip_group_check=True)
                        if c == 0 and t == 0 and half == 0:
                            mm.then_inc(up_free, 1)
                if c == 1:
                    mm.then_inc(down_free, 1)

            def bracket(start):
                for b in range(4):
                    mm = pe.matmul(bank[b][:, :], zeros_bf[:, 0:P], zeros_bf[:], start=start, stop=not start,
                                   skip_group_check=True)
                return mm

            with pe.Fori(0, DEPTH) as l:
                pe.wait_ge(acc_first, 1)
                mod_col(7, 0, 0)
                mod_col(7, 1, 1).then_inc(mod_cols, 1)
                turn_x(0, 0)
                for n in range(NW_IN):
                    for half in range(2):
                        if n == 1 and half == 1:
                            pe.wait_ge(mcol_ready, 1)
                        w_step(l, n, half)
                    if n == 7:
                        turn_latents()
                        turn_gates()
                    if n == 9:
                        project_latents()
                    if n == 11:
                        turn_diff()
                        turn_rows()
                turn_qk()
                gate_rows()
                for m in range(NMAP + 3):
                    if m < NMAP:
                        scores(m).then_inc(s_done, 1)
                    if 2 <= m < NMAP + 2:
                        turn_probs(m - 2)
                    if m >= 3:
                        values(m - 3)
                for n in range(3):
                    turn_y(n)
                for s in range(W_OUT_TILES):
                    w_out_step(l, s)
                turn_x(4, NT)
                router()
                bracket(True)
                expert_up(l, 0, 0)
                with pe.Fori(0, N_EXP // 2 - 1) as i:
                    for s in range(4):
                        if s % 2 == 0:
                            expert_gate(i, s // 2)
                        if s < 3:
                            expert_up(l, i, s + 1)
                        else:
                            expert_up(l, i + 1, 0)
                        expert_down(l, i, s)
                last = N_EXP // 2 - 1
                for s in range(4):
                    if s % 2 == 0:
                        expert_gate(last, s // 2)
                    if s < 3:
                        expert_up(l, last, s + 1)
                    expert_down(l, last, s)
                bracket(False).then_inc(moe_done, 1)
                end_of_layer(pe, l)


_INS = ["x", "c", "w_ada", "b_ada", "w_in", "mla_g_q", "mla_g_kv", "mla_w_uq", "mla_w_ukv", "ml_b_i", "ml_b_f",
        "sc_w", "df_lq1", "df_lk1", "df_lq2", "df_lk2", "df_g", "w_out", "ln1_g", "ln1_b", "w_router", "b_router",
        "w1", "w3", "w2", "ln2_g", "ln2_b"]


def kernel(**inputs):
    import concourse.bacc as _bacc
    from concourse.bass_utils import run_bass_kernel_spmd as _run

    nc = _bacc.Bacc("TRN2", target_bir_lowering=False, num_devices=1, dynamic_dma_scratch_size=1024)
    arrays = {f"in_{name}": np.ascontiguousarray(inputs[name]) for name in _INS}
    arrays["in_const"], arrays["in_ident_mask"], arrays["in_head_sel"] = shape_constants()
    aps = {}
    for name, arr in arrays.items():
        aps[name[3:]] = nc.dram_tensor(name, arr.shape, mybir.dt.from_np(arr.dtype), kind="ExternalInput").ap()
    out = nc.dram_tensor("out_0", (1, S, D), F32, kind="ExternalOutput").ap()
    build(nc, aps, out)
    r = _run(nc, [arrays], core_ids=[0])
    return r.results[0]["out_0"]
```

```python
import math
from contextlib import ExitStack

import concourse.bass as bass
import numpy as np
from concourse import mybir

F32 = mybir.dt.float32
F32R = mybir.dt.float32r
BF16 = mybir.dt.bfloat16
I32 = mybir.dt.int32
ENG = mybir.EngineType
ALU = mybir.AluOpType
ACT = mybir.ActivationFunctionType
AX = mybir.AxisListType

P = 128
D = 1024
S = 256
NT = S // P
KC = D // P
DEPTH = 2
Q_LORA, KV_LORA, ROPE, NOPE = 192, 128, 32, 64
QK = NOPE + ROPE
NH = 4
DV = 64
DK = 32
GW = 256
N_EXP, N_GRP = 16, 4
MOD_W = 32
F_EXP = 256
ALPHA = (2 * DEPTH) ** 0.25
LN_EPS = 1e-5
RMS_EPS = 1e-6
NEG = -1e30

W_IN_TILES = [(0, 256, "a"), (256, 96, "a2"), (2152, 256, "dq"), (2408, 256, "dk"), (2664, 256, "dv"),
              (1120, 264, "gates_o"), (864, 256, "mv"), (352, 256, "mq"), (608, 256, "mk"),
              (1384, 256, "cb"), (1640, 256, "cc"), (1896, 256, "ch")]
NW_IN = len(W_IN_TILES)
W_WIDTH = 264
W_SLOTS = 4
W_HI = 3
W_OUT_TILES = 4
W_TILES = NW_IN + W_OUT_TILES
E_SLOTS = 6
E_WORDS = KC * F_EXP
ADA_W = 1024
ADA_SLOTS = 3
ADA_COLS = 6 * D
ADA_TILES = KC * ADA_COLS // ADA_W
ADA_FIRST = KC * 2 * D // ADA_W
ADA_BETWEEN = {n: range(2 * (n - 1), 2 * n if n < NW_IN - 1 else ADA_TILES - ADA_FIRST) for n in range(1, NW_IN)}
ADA_AHEAD = 4
ADA_LATE = 2 * KC - 2 * ADA_AHEAD

COUNTS = 64
CAP = P
MOE_WORDS = (N_GRP * KC * CAP, N_GRP * D, 2 * S, 2 * S, 2 * S, 2 * S)
N_ARENA = 11080

C_GQ, C_GKV, C_DFG, C_L, C_BI, C_BF, C_SC = 0, 192, 320, 384, 512, 513, 514
N_CUR = 520
K_COS, K_SIN, K_PRIO, K_LI = 0, 2 * ROPE, 4 * ROPE, 4 * ROPE + N_EXP
K_IOTA = K_LI + 2 * DEPTH
N_CONST = K_IOTA + P


def lambda_init(l):
    return 0.8 - 0.6 * math.exp(-0.3 * l)


def shape_constants():
    inv = (1.0 / (np.float32(10000.0) ** (np.arange(0, ROPE, 2, dtype=np.float32) / np.float32(ROPE)))).astype(np.float32)
    ang = np.arange(S, dtype=np.float32)[:, None] * inv[None, :]
    cos, sin = np.cos(ang).astype(np.float32), np.sin(ang).astype(np.float32)
    c = np.zeros((P, N_CONST), np.float32)
    for t in range(NT):
        c[:, K_COS + t * ROPE:K_COS + (t + 1) * ROPE] = np.concatenate([cos, cos], 1)[t * P:(t + 1) * P]
        c[:, K_SIN + t * ROPE:K_SIN + (t + 1) * ROPE] = np.concatenate([-sin, sin], 1)[t * P:(t + 1) * P]
    c[:, K_PRIO:K_PRIO + N_EXP] = np.arange(N_EXP, 0, -1)
    for l in range(DEPTH):
        c[:, K_LI + l] = lambda_init(l)
        c[:, K_LI + DEPTH + l] = 1.0 - lambda_init(l)
    c[:, K_IOTA:K_IOTA + P] = np.arange(P)
    m = np.zeros((P, 2 * P), np.float32)
    m[:, 0:P] = np.eye(P)
    m[:, P:] = np.where(np.arange(P)[None, :] > np.arange(P)[:, None], np.float32(NEG), np.float32(0))
    sel = np.zeros((NH, NH, P), np.float32)
    for h in range(NH):
        sel[h, h] = 1.0
    return c, m, sel.reshape(NH, NH * P)


def build(nc, a, out):
    ctx = ExitStack()
    with ctx:
        def sb(name, shape, dt=F32):
            return ctx.enter_context(nc.sbuf_tensor(name, shape, dt))

        def sem(name):
            return ctx.enter_context(nc.semaphore(name))

        bank = [ctx.enter_context(nc.psum_tensor(f"bank{i}", [P, 512], F32)) for i in range(8)]
        w_bytes, e_bytes, u_bytes = 4 * KC * W_WIDTH, 4 * E_WORDS, 4 * KC * S
        w_at = -(-nc.sbuf_base // 32) * 32
        e_at = w_at + W_SLOTS * w_bytes
        e_end = max(e_at + E_SLOTS * e_bytes, e_at + 3 * e_bytes + W_HI * w_bytes)
        u_at, gate_at = e_end, e_end + u_bytes
        sb("stretch", [P, (gate_at + u_bytes - nc.sbuf_base + 31) // 4 + 1])

        def at(name, shape, offset, dt=F32):
            return nc.alloc_sbuf_tensor_at(name, shape, dt, offset=offset)

        w_ring = [at(f"w_ring{i}", [P, KC, W_WIDTH], w_at + i * w_bytes) for i in range(W_SLOTS)]
        w_lo = [at(f"w_lo{i}", [P, KC, W_WIDTH], w_at + i * w_bytes, F32R) for i in range(W_SLOTS)]
        e_ring = [at(f"e_ring{i}", [P, E_WORDS], e_at + i * e_bytes) for i in range(E_SLOTS)]
        w_hi = [at(f"w_hi{i}", [P, KC, W_WIDTH], e_at + 3 * e_bytes + i * w_bytes, F32R) for i in range(W_HI)]
        uT = at("uT", [P, KC, S], u_at)
        u_hi = at("u_hi", [P, KC, S], u_at, F32R)
        gate_row = at("gate_row", [P, 2, D], gate_at)
        u_lo = at("u_lo", [P, KC, S], gate_at, F32R)
        ada_ring = [sb(f"ada_ring{i}", [P, ADA_W]) for i in range(ADA_SLOTS)]
        mod_acc = sb("mod_acc", [P, ADA_COLS])
        x_sb = sb("x_sb", [P, NT, D])
        ln_gb = sb("ln_gb", [P, 2, D])
        cur = sb("cur", [P, N_CUR])
        const = sb("const", [P, N_CONST])
        ident_mask = sb("ident_mask", [P, 2 * P])
        im_bf = sb("im_bf", [P, 2 * P], BF16)
        zeros_bf = sb("zeros_bf", [P, 512], BF16)
        ones = sb("ones", [P, P])
        ones_s = sb("ones_s", [NH, S])
        head_sel = sb("head_sel", [NH, NH * P])
        w_rt = sb("w_rt", [P, KC, N_EXP])
        b_rt = sb("b_rt", [P, N_EXP])
        c_col = sb("c_col", [P, KC])
        mcol = sb("mcol", [P, 2, 2, KC])
        st = sb("st", [P, NT, 2, 6])
        mv = sb("mv", [P, NT, 2])
        var = sb("var", [P, 8])
        rstd = sb("rstd", [P, 8])
        neg_half = sb("neg_half", [P, 8])
        arena = sb("arena", [P, N_ARENA])
        arena_used = [0]

        def attention_buffer(*dims):
            lo = arena_used[0]
            arena_used[0] += math.prod(dims)
            flat = arena[:, lo:arena_used[0]]
            if len(dims) == 1:
                return flat
            names = "abc"[:len(dims)]
            return flat.rearrange(f"p ({' '.join(names)}) -> p {' '.join(names)}", **dict(zip(names, dims)))

        uq = sb("uq", [P, NH * QK])
        uq_b = sb("uq_b", [Q_LORA - P, NH * QK])
        ukv = sb("ukv", [P, NH * 2 * DV])
        zA = attention_buffer(NT, 352)
        zD = attention_buffer(NT, 768)
        zG = sb("zG", [P, NT, 8])
        sig_o = attention_buffer(NT, GW)
        m_v = attention_buffer(NT, GW)
        mqT = attention_buffer(2, S)
        mkT = attention_buffer(2, S)
        conv_at = arena_used[0]
        conv = attention_buffer(1540)
        cbT = attention_buffer(2, S)
        tmp = sb("tmp", [P, 2 * D])
        kvn = attention_buffer(NT, NH * 2 * DV)
        qf = attention_buffer(NT, NH * QK)
        kf = attention_buffer(NT, NH * QK)
        dT = attention_buffer(4, S)
        prob = attention_buffer(3, 384)
        rows = sb("rows", [NH, 4, S])
        nr_em = sb("nr_em", [P, 2, NT, NH])
        nmax = sb("nmax", [P, 12, NT])
        ssum = sb("ssum", [P, 12, NT])
        den = sb("den", [P, NT, NH])
        rden = sb("rden", [P, NT, NH])
        lam = sb("lam", [P, 8])
        score = sb("score", [P, NT, N_EXP])
        gates = sb("gates", [P, NT, N_EXP])
        rt = sb("rt", [P, 320])
        group_bf = sb("group_bf", [P, NT, N_GRP], BF16)
        before_bf = sb("before_bf", [P, P], BF16)
        ones_bf = sb("ones_bf", [P, P], BF16)
        path = sb("path", [1, 1], I32)

        ident = ident_mask[:, 0:P]
        ones_row = ones_s[:, :]
        ident_bf = im_bf[:, 0:P]
        mask_bf = im_bf[:, P:2 * P]
        ccT = conv[:, 0:512].rearrange("p (c s) -> p c s", c=2)
        chT = conv[:, 512:1024].rearrange("p (c s) -> p c s", c=2)
        cuT = conv[:, 1024:1540].rearrange("p (c s) -> p c s", c=2)
        u_raw = arena[:, conv_at:conv_at + KC * S].rearrange("p (k s) -> p k s", k=KC)
        yN = conv[:, 0:1536].rearrange("p (t n) -> p t n", t=NT)
        xn = tmp[:, :].rearrange("p (t n) -> p t n", t=NT)
        t1 = tmp[:, 0:D]
        t2 = tmp[:, D:2 * D]
        qfT = t1[0:QK, :].rearrange("p (h s) -> p h s", h=NH)
        kfT = t2[0:QK, :].rearrange("p (h s) -> p h s", h=NH)
        decay, probT = qf, kf
        conv_y = zA[:, :, :].rearrange("p t n -> p (t n)")[:, 0:512].rearrange("p (c s) -> p c s", c=2)
        pT0 = prob[:, :, :].rearrange("p a b -> p (a b)")[:, 0:512]
        pT1 = prob[:, :, :].rearrange("p a b -> p (a b)")[0:Q_LORA - P, 512:768]
        moe_at = [sum(MOE_WORDS[:q]) for q in range(len(MOE_WORDS) + 1)]
        assert moe_at[-1] <= N_ARENA and arena_used[0] <= N_ARENA
        uTs, yg, silu, sgate, hT, gmove = [arena[:, moe_at[q]:moe_at[q + 1]] for q in range(len(MOE_WORDS))]
        uTs = uTs.rearrange("p (k s) -> p k s", k=KC)
        yg = yg.rearrange("p (g n) -> p g n", g=N_GRP)
        silu, sgate, hT, gmove = [b.rearrange("p (s n) -> p s n", s=2) for b in (silu, sgate, hT, gmove)]
        to_slot = uT[:, 0:4, :].rearrange("p k s -> p (k s)").rearrange("p (t n) -> p t n", t=NT)
        from_slot = uT[:, 4:8, :].rearrange("p k s -> p (k s)").rearrange("p (t n) -> p t n", t=NT)

        def pair_rows(ap, n):
            return ap.unsqueeze(2).to_broadcast([P, ap.shape[1], n])

        c_in = sem("c_in")
        ident_in = sem("ident_in")
        const_in = sem("const_in")
        x_in = sem("x_in")
        setup = sem("setup")
        im_ready = sem("im_ready")
        c_ready = sem("c_ready")
        acc_zero = sem("acc_zero")
        acc_bias = sem("acc_bias")
        acc_bias_rest = sem("acc_bias_rest")
        w_in_sem = [sem(f"w_loaded{i}") for i in range(W_SLOTS)]
        w_free = sem("w_free")
        e_in_sem = [sem(f"e_loaded{i}") for i in range(E_SLOTS)]
        up_free = sem("up_free")
        down_free = sem("down_free")
        ada_in_sem = [sem(f"ada_loaded{i}") for i in range(ADA_SLOTS)]
        ada_free = sem("ada_free")
        small_in = sem("small_in")
        ln_in = sem("ln_in")
        entry_var, entry_rstd, entry_ready = sem("entry_var"), sem("entry_rstd"), sem("entry_ready")
        entry_chain = sem("entry_chain")
        layer_fin = sem("layer_fin")
        layer_go = sem("layer_go")
        tick = sem("tick")
        out_done = sem("out_done")

        layer_sems = []

        def lsem(name):
            s = sem(name)
            layer_sems.append(s)
            return s

        v = lsem("vector_chain")
        ac = lsem("scalar_chain")
        acc_first, acc_rest = lsem("acc_first"), lsem("acc_rest")
        mod_cols, mcol_ready = lsem("mod_cols"), lsem("mcol_ready")
        var_ready, rstd_ready, xn_ready = lsem("var_ready"), lsem("rstd_ready"), lsem("xn_ready")
        xt_done, ut_act, ut_dve = lsem("xt_done"), lsem("ut_act"), lsem("ut_dve")
        hi_ready, lo_ready, u_split = lsem("hi_ready"), lsem("lo_ready"), lsem("u_split")
        z_done, z_out = lsem("z_done"), lsem("z_out")
        lat_ready, lat_t, lat_act, lat_dve = lsem("lat_ready"), lsem("lat_t"), lsem("lat_act"), lsem("lat_dve")
        gate_t = lsem("gate_t")
        f_ready, lf_ready, rows_ready, rows_t, rows_out = (lsem("f_ready"), lsem("lf_ready"), lsem("rows_ready"),
                                                           lsem("rows_t"), lsem("rows_out"))
        proj_done, q_out, kv_out = lsem("proj_done"), lsem("q_out"), lsem("kv_out")
        d_roped, d_t, d_out = lsem("d_roped"), lsem("d_t"), lsem("d_out")
        qk_ready, qk_t, qT_out, kT_out = lsem("qk_ready"), lsem("qk_t"), lsem("qT_out"), lsem("kT_out")
        lam_dots, lam_exp = lsem("lam_dots"), lsem("lam_exp")
        rows_g, rows_g_out, cols2 = lsem("rows_g"), lsem("rows_g_out"), lsem("cols2")
        s_done, max_ready, p_act, p_dve = lsem("s_done"), lsem("max_ready"), lsem("p_act"), lsem("p_dve")
        decay_ready, pt_done, pt_out, pv_done = lsem("decay_ready"), lsem("pt_done"), lsem("pt_out"), lsem("pv_done")
        o_read = lsem("o_read")
        y_ready, y_t, y_out_act, conv_ready = lsem("y_ready"), lsem("y_t"), lsem("y_out_act"), lsem("conv_ready")
        mix_done, ln1_used = lsem("mix_done"), lsem("ln1_used")
        logits, score_ready = lsem("logits"), lsem("score_ready")
        diag_ready, g_ready, h_done, silu_done, h_ready, y_step, sg_done = (
            lsem("diag_ready"), lsem("g_ready"), lsem("h_done"), lsem("silu_done"), lsem("h_ready"),
            lsem("y_step"), lsem("sg_done"))
        moe_done, x_done = lsem("moe_done"), lsem("x_done")
        group_ready, ranks, path_ready, to_slot_ready = (lsem("group_ready"), lsem("ranks"), lsem("path_ready"),
                                                         lsem("to_slot_ready"))
        sorted_done, us_act = lsem("sorted_done"), lsem("us_act")
        turned_back, from_act, from_dve = lsem("turned_back"), lsem("from_act"), lsem("from_dve")
        yg_done, yg_act, yg_dve = lsem("yg_done"), lsem("yg_act"), lsem("yg_dve")
        first_layer_sem = min(s.num for s in layer_sems)
        last_layer_sem = max(s.num for s in layer_sems)
        assert last_layer_sem - first_layer_sem + 1 == len(layer_sems)

        block = ctx.enter_context(nc.Block())

        NMAP = 16

        def end_of_layer(eng, l):
            eng.drain().then_inc(layer_fin, 1)
            eng.wait_ge(layer_go, l + 2)

        @block.sync
        def _(sp):
            sp.dma_start(c_col[:], a["c"].rearrange("b (p k) -> (b p) k", k=KC)).then_inc(c_in, 16)
            sp.dma_start(x_sb[:], a["x"].rearrange("b (t p) d -> (b p) t d", p=P)).then_inc(x_in, 16)
            sp.dma_start(ident_mask[:], a["ident_mask"]).then_inc(ident_in, 16)

            ada = a["w_ada"].rearrange("l (p k) n -> l k p n", k=KC)

            def load_ada(l, k, m, slot, nth):
                sp.wait_ge(ada_free, nth + 1)
                sp.dma_start(ada_ring[slot][:], ada[l, k, :, m * ADA_W:(m + 1) * ADA_W]).then_inc(ada_in_sem[slot], 16)

            def load_w(l, n):
                sp.wait_ge(w_free, l * W_TILES + n + 1)
                if n < NW_IN:
                    c0, width, _ = W_IN_TILES[n]
                    src = a["w_in"].rearrange("l (p k) n -> l p k n", k=KC)[l, :, :, c0:c0 + width]
                else:
                    width = D // W_OUT_TILES
                    c0 = (n - NW_IN) * width
                    src = a["w_out"].rearrange("l (k p) n -> l p k n", p=P)[l, :, :, c0:c0 + width]
                sp.dma_start(w_ring[n % W_SLOTS][:, :, 0:width], src).then_inc(w_in_sem[n % W_SLOTS], 16)

            for n in range(ADA_FIRST):
                if n == ADA_FIRST - ADA_SLOTS:
                    load_w(0, 0)
                load_ada(0, n // 2, n % 2, n % ADA_SLOTS, n)
            sp.dma_start(const[:], a["const"]).then_inc(const_in, 16)
            sp.dma_start(head_sel[:], a["head_sel"]).then_inc(const_in, 16)
            sp.dma_start(w_rt[:], a["w_router"].rearrange("(p k) n -> p k n", k=KC)).then_inc(const_in, 16)
            sp.dma_start(b_rt[:], a["b_router"].unsqueeze(0).to_broadcast([P, N_EXP])).then_inc(const_in, 16)

            def load_expert(l, i, j):
                e = 2 * i + j
                sp.wait_ge(up_free, l * N_EXP + e + 1)
                for q, name in enumerate(("w1", "w3")):
                    sp.dma_start(e_ring[3 * j + q][:].rearrange("p (k f) -> p k f", k=KC),
                                 a[name].rearrange("l e (p k) f -> l e p k f", k=KC)[l, e]).then_inc(
                        e_in_sem[3 * j + q], 16)
                sp.wait_ge(down_free, l * N_EXP + e + 1)
                sp.dma_start(e_ring[3 * j + 2][:].rearrange("p (c n) -> p c n", c=2),
                             a["w2"].rearrange("l e (c p) n -> l e p c n", p=P)[l, e]).then_inc(
                    e_in_sem[3 * j + 2], 16)

            def load_next_ada(l, k, half):
                after = nc.s_assert_within(l + 1, 1, DEPTH - 1)
                for m in range(3 * half, 3 * half + 3):
                    load_ada(after, k, m, m % ADA_SLOTS, (l + 1) * ADA_TILES + 6 * k + m)

            with sp.Fori(0, DEPTH) as l:
                with sp.If(l > 0):
                    load_w(l, 0)
                for n in range(1, W_TILES):
                    load_w(l, n)
                    if n in ADA_BETWEEN:
                        with sp.If(l < 1):
                            for q in ADA_BETWEEN[n]:
                                load_ada(0, q // 4, 2 + q % 4, (ADA_FIRST + q) % ADA_SLOTS, ADA_FIRST + q)
                for j in range(2):
                    if j == 1:
                        sp.wait_ge(w_free, l * W_TILES + (W_SLOTS + NW_IN))
                    load_expert(l, 0, j)
                    with sp.If(l < DEPTH - 1):
                        for b in range(j * ADA_AHEAD, (j + 1) * ADA_AHEAD):
                            load_next_ada(l, b // 2, b % 2)
                with sp.Fori(1, 1 + ADA_LATE // 2) as i:
                    for j in range(2):
                        with sp.If(l < DEPTH - 1):
                            load_next_ada(l, i + (ADA_AHEAD - 1), j)
                        load_expert(l, i, j)
                with sp.Fori(1 + ADA_LATE // 2, N_EXP // 2) as i:
                    for j in range(2):
                        load_expert(l, i, j)
            sp.wait_ge(out_done, 16 * NT)

        @block.gpsimd
        def _(pool):
            nc.gpsimd.memset(mod_acc[:, 0:2 * D], 0.0).then_inc(acc_zero, 1)
            nc.gpsimd.memset(mod_acc[:, 2 * D:], 0.0).then_inc(acc_zero, 1)
            nc.gpsimd.memset(ones_bf[:], 1.0).then_inc(setup, 1)
            nc.gpsimd.memset(ones[:], 1.0).then_inc(setup, 1)
            nc.gpsimd.memset(zeros_bf[:], 0.0).then_inc(setup, 1)
            nc.gpsimd.memset(ones_s[:], 1.0)
            nc.gpsimd.memset(neg_half[:], -0.5).then_inc(setup, 1)
            nc.gpsimd.sem_inc(layer_go, 1)
            pool.wait_ge(setup, 4)

            def root(n, cols):
                pool.wait_ge(var_ready, n)
                nc.gpsimd.tensor_tensor(rstd[:, cols], var[:, cols], neg_half[:, cols], ALU.pow).then_inc(rstd_ready, 1)

            def entry_root(n, t):
                pool.wait_ge(entry_var, n)
                nc.gpsimd.tensor_tensor(rstd[:, t:t + 1], var[:, t:t + 1], neg_half[:, t:t + 1],
                                        ALU.pow).then_inc(entry_rstd, 1)

            for t in range(NT):
                entry_root(t + 1, t)
            with pool.Fori(0, DEPTH) as l:
                for n in range(NW_IN):
                    pool.wait_ge(hi_ready, n + 1)
                    cols = (slice(None), slice(None), slice(0, W_IN_TILES[n][1]))
                    nc.gpsimd.tensor_tensor(w_lo[n % W_SLOTS][cols], w_ring[n % W_SLOTS][cols],
                                            w_hi[n % W_HI][:].bitcast(F32)[cols], ALU.subtract).then_inc(lo_ready, 1)
                    if n == 5:
                        root(1, slice(0, 4))
                with pool.If(l < DEPTH - 1):
                    pool.wait_ge(cols2, 1)
                    nc.gpsimd.memset(mod_acc[:], 0.0).then_inc(acc_zero, 1)
                root(2, slice(0, 8))
                for t in range(NT):
                    root(3 + 2 * t, slice(t, t + 1))
                    root(4 + 2 * t, slice(t, t + 1))
                for t in range(NT):
                    root(7 + t, slice(t, t + 1))
                    with pool.If(l < DEPTH - 1):
                        entry_root(NT * (l + 1) + (t + 1), t)
                pool.drain().then_inc(layer_fin, 1)
                pool.wait_ge(layer_fin, 4 * (l + 1))
                nc.gpsimd.sem_inc(tick, 1)
                nc.gpsimd.sem_clear(range(first_layer_sem, last_layer_sem + 1))
                nc.gpsimd.sem_inc(layer_go, 1)

        @block.scalar
        def _(act):
            act.wait_ge(acc_zero, 1)
            act.dma_start(mod_acc[0:1, 0:2 * D], a["b_ada"][0:1, 0:2 * D]).then_inc(acc_bias, 16)
            act.wait_ge(c_in, 16)
            nc.scalar.activation(c_col[:], c_col[:], ACT.Silu).then_inc(c_ready, 1)
            act.wait_ge(acc_zero, 2)
            act.dma_start(mod_acc[0:1, 2 * D:], a["b_ada"][0:1, 2 * D:]).then_inc(acc_bias_rest, 16)

            def high_part(l, n):
                act.wait_ge(w_in_sem[n % W_SLOTS], 16 * (l * (W_TILES // W_SLOTS) + n // W_SLOTS + 1))
                if n >= W_HI:
                    act.wait_ge(z_done, 2 * (n - W_HI) + 2)
                width = W_IN_TILES[n][1]
                nc.scalar.activation(w_hi[n % W_HI][:, :, 0:width], w_ring[n % W_SLOTS][:, :, 0:width],
                                     ACT.Copy).then_inc(hi_ready, 1)

            def evict_x(first_bank, cols):
                for t in range(NT):
                    for k in range(KC if t == 0 and cols == 1 else KC // 2):
                        act.wait_ge(xt_done, (cols * NT + t) * KC + 4 * (k // 4) + 4)
                        act.wait_ge(mcol_ready, cols + 1)
                        c0 = (k % 4) * P
                        for dst in ((u_raw, u_hi) if cols == 0 else (uT,)):
                            ins = nc.scalar.activation(dst[:, k, t * P:(t + 1) * P],
                                                       bank[first_bank + 2 * t + k // 4][:, c0:c0 + P], ACT.Identity,
                                                       bias=mcol[:, cols, 0, k:k + 1], scale=mcol[:, cols, 1, k:k + 1])
                        ins.then_inc(ut_act, 1)

            with act.Fori(0, DEPTH) as l:
                high_part(l, 0)
                evict_x(0, 0)
                for n in range(1, W_HI):
                    high_part(l, n)

                def param(dst, src):
                    act.dma_start(dst, src).then_inc(small_in, 16)

                def row_param(c0, name, n):
                    param(cur[:, c0:c0 + n], a[name][bass.ds(l, 1), :].to_broadcast([P, n]))

                row_param(C_GQ, "mla_g_q", Q_LORA)
                row_param(C_GKV, "mla_g_kv", KV_LORA)
                row_param(C_DFG, "df_g", DV)
                for q, name in enumerate(("df_lq1", "df_lk1", "df_lq2", "df_lk2")):
                    row_param(C_L + q * DK, name, DK)
                with nc.allow_non_contiguous_dma(reason="a few words to a partition each"):
                    param(cur[0:NH, C_BI:C_BI + 1], a["ml_b_i"][bass.ds(l, 1), :].rearrange("a h -> h a"))
                    param(cur[0:NH, C_BF:C_BF + 1], a["ml_b_f"][bass.ds(l, 1), :].rearrange("a h -> h a"))
                    for c in range(2):
                        param(cur[:, C_SC + 3 * c:C_SC + 3 * c + 3],
                              a["sc_w"][bass.ds(l, 1), :, c * P:(c + 1) * P].rearrange("a w p -> (a p) w"))
                param(uq[:], a["mla_w_uq"][l, 0:P, :])
                param(uq_b[:], a["mla_w_uq"][l, P:Q_LORA, :])
                param(ukv[:], a["mla_w_ukv"][l])

                def ln_load(row, name):
                    act.dma_start(ln_gb[:, row, :], a[name][bass.ds(l, 1), :].to_broadcast([P, D])).then_inc(ln_in, 16)

                dest = {
                    "a": lambda t: (zA[:, t, 0:256], 1.0), "a2": lambda t: (zA[:, t, 256:352], 1.0),
                    "dq": lambda t: (zD[:, t, 0:256], DK ** -0.5), "dk": lambda t: (zD[:, t, 256:512], 1.0),
                    "dv": lambda t: (zD[:, t, 512:768], 1.0), "mv": lambda t: (m_v[:, t, :], 1.0),
                    "mq": lambda c: (mqT[:, c, :], DV ** -0.5), "mk": lambda c: (mkT[:, c, :], 1.0),
                    "cb": lambda c: (cbT[:, c, :], 1.0), "cc": lambda c: (ccT[:, c, :], 1.0),
                    "ch": lambda c: (chT[:, c, :], 1.0)}
                def latents_out():
                    act.wait_ge(lat_t, 1)
                    nc.scalar.activation(pT0, bank[0][:, :], ACT.Copy).then_inc(lat_act, 1)

                def log_gates():
                    act.wait_ge(f_ready, 1)
                    nc.scalar.activation(rows[:, 1, :], rows[:, 1, :], ACT.Exp).then_inc(ac, 1)
                    act.wait_ge(ac, 1)
                    nc.scalar.activation(rows[:, 1, :], rows[:, 1, :], ACT.Ln, bias=1.0).then_inc(lf_ready, 1)

                def queries_out():
                    for t in range(NT):
                        act.wait_ge(proj_done, t + 1)
                        nc.scalar.activation(qf[:, t, :], bank[3 if t == 0 else 1][:, 0:NH * QK], ACT.Copy,
                                             scale=QK ** -0.5).then_inc(q_out, 1)

                def d_out_all():
                    for t in range(NT):
                        act.wait_ge(d_t, t + 1)
                        nc.scalar.activation(dT[:, :, t * P:(t + 1) * P],
                                             bank[t][:, :].rearrange("p (b s) -> p b s", b=4), ACT.Copy).then_inc(d_out, 1)

                for n, (_, width, kind) in enumerate(W_IN_TILES):
                    for half in range(2):
                        step = 2 * n + half
                        src = bank[4 + step % 4]
                        act.wait_ge(z_done, step + 1)
                        if kind == "gates_o":
                            nc.scalar.activation(zG[:, half, :], src[:, 0:8], ACT.Copy)
                            nc.scalar.activation(sig_o[:, half, :], src[:, 8:264], ACT.Sigmoid).then_inc(z_out, 1)
                        else:
                            dst, scale = dest[kind](half)
                            nc.scalar.activation(dst, src[:, 0:width], ACT.Copy, scale=scale).then_inc(z_out, 1)
                    if n + W_HI < NW_IN:
                        high_part(l, n + W_HI)
                    if n == 7:
                        latents_out()
                    if n == 8:
                        log_gates()
                    if n == 9:
                        queries_out()
                    if n == 11:
                        d_out_all()

                ln_load(0, "ln1_g")
                ln_load(1, "ln1_b")
                act.wait_ge(lam_dots, 1)
                nc.scalar.activation(lam[:, 2:4], lam[:, 0:2], ACT.Exp).then_inc(lam_exp, 1)
                act.wait_ge(rows_t, 1)
                nc.scalar.activation(nr_em[:, 1, :, :], bank[3][:, 8:16].rearrange("p (t h) -> p t h", t=NT), ACT.Exp,
                                     scale=-1.0)
                nc.scalar.activation(nr_em[:, 0, :, :], bank[3][:, 0:8].rearrange("p (t h) -> p t h", t=NT), ACT.Copy,
                                     scale=-1.0).then_inc(rows_out, 1)
                for t in range(NT):
                    act.wait_ge(qk_t, t + 1)
                    nc.scalar.activation(qfT[:, :, t * P:(t + 1) * P],
                                         bank[2 + t][0:QK, :].rearrange("p (h s) -> p h s", h=NH), ACT.Copy).then_inc(qT_out, 1)
                for m in range(NMAP):
                    if m == 2:
                        for g in range(2):
                            for half in range(2):
                                act.wait_ge(rows_g, 2 * g + half + 1)
                                nc.scalar.activation(gate_row[:, g, half * 512:(half + 1) * 512], bank[4 + 2 * g + half][:, :],
                                                     ACT.Copy).then_inc(rows_g_out, 1)
                    act.wait_ge(s_done, m + 1)
                    if m < 12:
                        src = bank[m % 4]
                        act.wait_ge(max_ready, m + 1)
                        if m >= 3:
                            act.wait_ge(pt_done, m - 2)
                        nc.scalar.activation(prob[:, m % 3, 0:P], src[:, 0:P], ACT.Exp, bias=nmax[:, m, 0:1],
                                             accum_out=ssum[:, m, 0:1])
                        nc.scalar.activation(prob[:, m % 3, P:384], src[:, P:384], ACT.Exp, bias=nmax[:, m, 1:2],
                                             accum_out=ssum[:, m, 1:2]).then_inc(p_act, 1)
                    else:
                        h = m - 12
                        src = bank[2 * (h % 2)]
                        if h == 0:
                            act.wait_ge(rows_out, 1)
                        if h >= 2:
                            act.wait_ge(p_dve, h - 1)
                        nc.scalar.activation(decay[:, h % 2, 0:P], src[:, 0:P], ACT.Exp, bias=nr_em[:, 0, 0, h:h + 1])
                        nc.scalar.activation(decay[:, h % 2, P:384], src[:, P:384], ACT.Exp,
                                             bias=nr_em[:, 0, 1, h:h + 1]).then_inc(decay_ready, 1)

                with act.If(l < DEPTH - 1):
                    act.wait_ge(acc_zero, l + 3)
                    after = nc.s_assert_within(l + 1, 1, DEPTH - 1)
                    act.dma_start(mod_acc[0:1, :], a["b_ada"][bass.ds(after, 1), :]).then_inc(acc_bias, 16)
                for n, (b, c0) in enumerate(((4, 0), (5, 6), (6, 2))):
                    act.wait_ge(y_t, n + 1)
                    nc.scalar.activation(uT[:, c0:c0 + 2, :], bank[b][:, :].rearrange("p (c s) -> p c s", c=2),
                                         ACT.Copy).then_inc(y_out_act, 1)
                evict_x(4, 1)
                act.wait_ge(ln1_used, 1)
                ln_load(0, "ln2_g")
                ln_load(1, "ln2_b")
                act.wait_ge(logits, NT)
                nc.scalar.activation(score[:], bank[0][:, 0:NT * N_EXP].rearrange("p (t e) -> p t e", t=NT),
                                     ACT.Sigmoid).then_inc(score_ready, 1)
                act.wait_ge(path_ready, 1)
                crowded = nc.values_load(path[0:1, 0:1], engines=[ENG.Activation], min_val=0, max_val=1)
                with act.If(crowded < 1):
                    for k in range(KC):
                        act.wait_ge(sorted_done, k + 1)
                        nc.scalar.activation(uTs[:, k, :], bank[k][:, :], ACT.Identity, bias=mcol[:, 1, 0, k:k + 1],
                                             scale=mcol[:, 1, 1, k:k + 1]).then_inc(us_act, 1)

                    def silu_out(g, j):
                        act.wait_ge(h_done, 4 * g + j + 1)
                        act.wait_ge(h_ready, 4 * g + j + 1)
                        nc.scalar.activation(silu[:, j % 2, :], bank[j % 2][:, 0:S], ACT.Silu).then_inc(silu_done, 1)

                    def group_out(g):
                        act.wait_ge(yg_done, g + 2)
                        nc.scalar.activation(yg[:, g, 0:512], bank[4][:, :], ACT.Copy).then_inc(yg_act, 1)

                    nc.scalar.sem_inc(yg_act, 1)
                    silu_out(0, 0)
                    act.wait_ge(turned_back, 1)
                    nc.scalar.activation(from_slot[:, 0, :], bank[6][:, :], ACT.Copy).then_inc(from_act, 1)
                    with act.Fori(0, N_GRP - 1) as g:
                        for j in range(1, 4):
                            silu_out(g, j)
                        silu_out(g + 1, 0)
                        group_out(g)
                    for j in range(1, 4):
                        silu_out(N_GRP - 1, j)
                    group_out(N_GRP - 1)
                with act.If(crowded > 0):
                    with act.Fori(0, N_EXP // 2) as i:
                        for s in range(4):
                            act.wait_ge(h_done, 4 * i + s + 1)
                            act.wait_ge(h_ready, 4 * i + s + 1)
                            nc.scalar.activation(silu[:, s % 2, :], bank[4 + s % 2][:, 0:S],
                                                 ACT.Silu).then_inc(silu_done, 1)
                with act.If(l > DEPTH - 2):
                    for t in range(NT):
                        act.wait_ge(x_done, t + 1)
                        act.dma_start(out[0, t * P:(t + 1) * P, :], x_sb[:, t, :]).then_inc(out_done, 16)
                end_of_layer(act, l)
            act.wait_ge(out_done, 16 * NT)

        @block.vector
        def _(dve):
            nc.vector.sem_inc(ada_free, ADA_SLOTS)
            V = nc.vector
            chain = [0]

            def link(ins):
                chain[0] += 1
                ins.then_inc(v, 1)
                dve.wait_ge(v, chain[0])

            def ada_step(slot, slot_round, k_col, m):
                dve.wait_ge(ada_in_sem[slot], 16 * slot_round)
                part = mod_acc[:, m * ADA_W:(m + 1) * ADA_W]
                V.scalar_tensor_tensor(out=part, in0=ada_ring[slot][:], scalar=k_col, in1=part,
                                       op0=ALU.mult, op1=ALU.add).then_inc(ada_free, 1)

            dve.wait_ge(ident_in, 16)
            V.tensor_copy(im_bf[:], ident_mask[:]).then_inc(im_ready, 1)
            V.tensor_scalar(before_bf[:], ident_mask[:, P:], 0.0, None, ALU.is_lt).then_inc(im_ready, 1)
            dve.wait_ge(x_in, 16)

            def statistics(t, half):
                V.bn_stats(st[:, t, half, :], x_sb[:, t, half * 512:(half + 1) * 512]).then_inc(v, 1)
                chain[0] += 1

            def variance(t):
                dve.wait_ge(v, chain[0])
                link(V.bn_aggr(mv[:, t, :], st[:, t, :, :].rearrange("p a b -> p (a b)")))
                V.tensor_scalar(var[:, t:t + 1], mv[:, t, 1:2], LN_EPS, None, ALU.add).then_inc(var_ready, 1)

            def normalise(t):
                return V.tensor_scalar(xn[:, t, :], x_sb[:, t, :], mv[:, t, 0:1], rstd[:, t:t + 1], ALU.subtract, ALU.mult)

            def evict_x(first_bank, cols, t):
                for k in range(KC // 2, KC):
                    dve.wait_ge(xt_done, (cols * NT + t + 1) * KC)
                    c0 = (k % 4) * P
                    for dst in ((u_raw, u_hi) if cols == 0 else (uT,)):
                        ins = V.tensor_scalar(dst[:, k, t * P:(t + 1) * P], bank[first_bank + 2 * t + k // 4][:, c0:c0 + P],
                                              mcol[:, cols, 1, k:k + 1], mcol[:, cols, 0, k:k + 1], ALU.mult, ALU.add)
                    ins.then_inc(ut_dve, 1)

            def mod_columns(cols, b):
                V.tensor_copy(mcol[:, cols, 0, :], bank[b][:, 0:KC * MOD_W:MOD_W])
                V.tensor_scalar(mcol[:, cols, 1, :], bank[b][:, KC * MOD_W:2 * KC * MOD_W:MOD_W], 1.0, None, ALU.add).then_inc(mcol_ready, 1)
                dve.wait_ge(mcol_ready, cols + 1)

            def rotate(src, dst, heads, dst_heads=None):
                n = NT * heads * ROPE
                h = ROPE // 2

                def table(c0, lo, hi):
                    return const[:, c0:c0 + NT * ROPE].rearrange("p (t r) -> p t r", t=NT)[:, :, lo:hi].unsqueeze(2).to_broadcast(
                        [P, NT, heads, hi - lo])
                r1 = t1[:, 0:n].rearrange("p (t h r) -> p t h r", t=NT, h=heads)
                r2 = t2[:, 0:n].rearrange("p (t h r) -> p t h r", t=NT, h=heads)
                V.tensor_tensor(r1, src, table(K_COS, 0, ROPE), ALU.mult)
                V.tensor_tensor(r2[:, :, :, 0:h], src[:, :, :, h:ROPE], table(K_SIN, 0, h), ALU.mult)
                link(V.tensor_tensor(r2[:, :, :, h:ROPE], src[:, :, :, 0:h], table(K_SIN, h, ROPE), ALU.mult))
                if dst_heads:
                    r1 = r1.to_broadcast([P, NT, dst_heads, ROPE])
                    r2 = r2.to_broadcast([P, NT, dst_heads, ROPE])
                return V.tensor_tensor(dst, r1, r2, ALU.add)

            def post_norm(t, gate, half_done, nth, ln_wait):
                for half in range(2):
                    half_done(t, half)
                    part = slice(half * 512, (half + 1) * 512)
                    link(V.tensor_tensor(xn[:, t, part], bank[2 * t + half][:, :], gate_row[:, gate, part], ALU.mult))
                    link(V.scalar_tensor_tensor(out=x_sb[:, t, part], in0=x_sb[:, t, part], scalar=ALPHA,
                                                in1=xn[:, t, part], op0=ALU.mult, op1=ALU.add))
                    statistics(t, half)
                variance(t)
                ln_wait()
                link(V.scalar_tensor_tensor(out=xn[:, t, :], in0=x_sb[:, t, :], scalar=mv[:, t, 0:1], in1=ln_gb[:, 0, :],
                                            op0=ALU.subtract, op1=ALU.mult))
                dve.wait_ge(rstd_ready, nth)
                return V.scalar_tensor_tensor(out=x_sb[:, t, :], in0=xn[:, t, :], scalar=rstd[:, t:t + 1],
                                              in1=ln_gb[:, 1, :], op0=ALU.mult, op1=ALU.add)

            def entry_variance(t, done):
                for half in range(2):
                    V.bn_stats(st[:, t, half, :], x_sb[:, t, half * 512:(half + 1) * 512]).then_inc(entry_chain, 1)
                dve.wait_ge(entry_chain, done + 2)
                nc.vector.sem_inc(tick, 1)
                V.bn_aggr(mv[:, t, :], st[:, t, :, :].rearrange("p a b -> p (a b)")).then_inc(entry_chain, 1)
                dve.wait_ge(entry_chain, done + 3)
                V.tensor_scalar(var[:, t:t + 1], mv[:, t, 1:2], LN_EPS, None, ALU.add).then_inc(entry_var, 1)

            for t in range(NT):
                entry_variance(t, 3 * t)
            for t in range(NT):
                dve.wait_ge(entry_rstd, t + 1)
                normalise(t).then_inc(entry_ready, 1)

            with dve.Fori(0, DEPTH) as l:
                chain[0] = 0
                with dve.If(l < 1):
                    dve.wait_ge(c_ready, 1)
                    dve.wait_ge(acc_bias, 16)
                    for n in range(ADA_FIRST):
                        if n >= 2:
                            dve.wait_ge(ada_free, ADA_SLOTS + n - 1)
                        ada_step(n % ADA_SLOTS, n // ADA_SLOTS + 1, c_col[:, n // 2:n // 2 + 1], n % 2)
                dve.drain().then_inc(acc_first, 1)
                dve.wait_ge(mod_cols, 1)
                mod_columns(0, 7)
                def low_part(t):
                    cols = (slice(None), slice(None), slice(t * P, (t + 1) * P))
                    V.tensor_tensor(u_lo[cols], u_raw[cols], u_hi[:].bitcast(F32)[cols], ALU.subtract).then_inc(u_split, 1)

                for t in range(NT):
                    evict_x(0, 0, t)
                    dve.wait_ge(ut_act, (t + 1) * KC // 2)
                    dve.wait_ge(ut_dve, (t + 1) * KC // 2)
                    low_part(t)

                def ada_rest(lo, hi):
                    with dve.If(l < 1):
                        if lo == 0:
                            dve.wait_ge(acc_bias_rest, 16)
                            nc.vector.sem_inc(tick, 1)
                        for q in range(lo, hi):
                            n = ADA_FIRST + q
                            if q >= 4:
                                dve.wait_ge(ada_free, ADA_SLOTS + n - 3)
                            ada_step(n % ADA_SLOTS, n // ADA_SLOTS + 1, c_col[:, q // 4:q // 4 + 1], 2 + q % 4)

                ada_rest(0, 6)
                with dve.If(l > 0):
                    dve.drain().then_inc(acc_rest, 1)
                dve.wait_ge(small_in, 16 * 14 * (l + 1))
                dve.wait_ge(z_out, 4)
                for t in range(NT):
                    for q, (c0, n) in enumerate(((0, Q_LORA), (Q_LORA, KV_LORA))):
                        z = zA[:, t, c0:c0 + n]
                        c1 = (2 * t + q) * Q_LORA
                        ins = V.tensor_tensor_reduce(out=t1[:, c1:c1 + n], in0=z, in1=z, scale=1.0 / n,
                                                     scalar=RMS_EPS, op0=ALU.mult, op1=ALU.add, accum_out=var[:, 2 * t + q:2 * t + q + 1])
                ins.then_inc(var_ready, 1)
                dve.wait_ge(var_ready, 1)
                dve.wait_ge(const_in, 16 * 4)
                rotate(zA[:, :, 320:352].unsqueeze(2), kf[:, :, :].rearrange("p t (h c) -> p t h c", h=NH)[:, :, :, NOPE:QK],
                       1, NH).then_inc(v, 1)
                chain[0] += 1
                ada_rest(6, 14)
                dve.wait_ge(rstd_ready, 1)
                for t in range(NT):
                    for q, (c0, n, g) in enumerate(((0, Q_LORA, C_GQ), (Q_LORA, KV_LORA, C_GKV))):
                        z = zA[:, t, c0:c0 + n]
                        ins = V.scalar_tensor_tensor(out=z, in0=z, scalar=rstd[:, 2 * t + q:2 * t + q + 1],
                                                     in1=cur[:, g:g + n], op0=ALU.mult, op1=ALU.mult)
                ins.then_inc(lat_ready, 1)
                for q in range(2):
                    c0 = C_L + 2 * q * DK
                    ins = V.tensor_tensor_reduce(out=rt[:, q * DK:(q + 1) * DK], in0=cur[:, c0:c0 + DK], in1=cur[:, c0 + DK:c0 + 2 * DK],
                                                 scale=1.0, scalar=0.0, op0=ALU.mult, op1=ALU.add, accum_out=lam[:, q:q + 1])
                ins.then_inc(lam_dots, 1)
                dve.wait_ge(z_out, 8)
                dve.wait_ge(v, chain[0])
                qk = zD[:, :, 0:512].rearrange("p t (h r) -> p t h r", h=16)
                rotate(qk, qk, 16).then_inc(d_roped, 1)
                ada_rest(14, 20)
                dve.wait_ge(lat_t, 2)
                V.tensor_copy(pT1, bank[1][0:Q_LORA - P, 0:S]).then_inc(lat_dve, 1)

                dve.wait_ge(gate_t, 1)
                link(V.tensor_scalar(rows[:, 0, :], bank[2][0:NH, S:2 * S], cur[0:NH, C_BF:C_BF + 1], None, ALU.add))
                link(V.tensor_scalar(rows[:, 1, :], rows[:, 0, :], -1.0, None, ALU.mult))
                V.tensor_tensor(rows[:, 1, :], rows[:, 0, :], rows[:, 1, :], ALU.min).then_inc(f_ready, 1)
                dve.wait_ge(lf_ready, 1)
                link(V.scalar_tensor_tensor(out=rows[:, 0, :], in0=rows[:, 0, :], scalar=0.0, in1=rows[:, 1, :],
                                            op0=ALU.min, op1=ALU.subtract))
                link(V.tensor_tensor_scan(rows[:, 2, :], ones_row, rows[:, 0, :], 0.0, ALU.mult, ALU.add))
                link(V.scalar_tensor_tensor(out=rows[:, 1, :], in0=bank[2][0:NH, 0:S], scalar=cur[0:NH, C_BI:C_BI + 1],
                                            in1=rows[:, 2, :], op0=ALU.add, op1=ALU.subtract))
                link(V.tensor_tensor_scan(rows[:, 3, :], ones_row, rows[:, 1, :], 0.0, ALU.mult, ALU.max))
                V.tensor_tensor(rows[:, 2, :], rows[:, 2, :], rows[:, 3, :], ALU.add).then_inc(rows_ready, 1)

                ada_rest(20, 23)
                for t in range(NT):
                    dve.wait_ge(proj_done, 3 + t)
                    V.tensor_copy(kvn[:, t, :], bank[0 if t == 0 else 2][:, :]).then_inc(kv_out, 1)
                dve.wait_ge(kv_out, NT)
                for t in range(NT):
                    V.tensor_copy(kf[:, t, :].rearrange("p (h c) -> p h c", h=NH)[:, :, 0:NOPE],
                                  kvn[:, t, :].rearrange("p (h c) -> p h c", h=NH)[:, :, 0:NOPE])
                dve.wait_ge(q_out, NT)
                qpe = qf[:, :, :].rearrange("p t (h c) -> p t h c", h=NH)[:, :, :, NOPE:QK]
                dve.wait_ge(d_roped, 1)
                rotate(qpe, qpe, NH).then_inc(qk_ready, 1)

                ada_rest(23, 26)
                dve.wait_ge(z_out, 24)
                dve.wait_ge(z_done, 24)
                V.memset(cuT[:, :, 0:2], 0.0)
                link(V.tensor_tensor(cuT[:, :, 2:S + 2], ccT, chT, ALU.mult))
                y = conv_y
                dve.wait_ge(qk_ready, 1)
                for tap in (2, 1, 0):
                    for c in range(2):
                        w = cur[:, C_SC + 3 * c + tap:C_SC + 3 * c + tap + 1]
                        src = cuT[:, c, tap:tap + S]
                        if tap == 2:
                            ins = V.tensor_scalar(y[:, c, :], src, w, None, ALU.mult)
                        else:
                            ins = V.scalar_tensor_tensor(out=y[:, c, :], in0=src, scalar=w, in1=y[:, c, :],
                                                         op0=ALU.mult, op1=ALU.add)
                        ins.then_inc(v, 1)
                        chain[0] += 1
                    dve.wait_ge(v, chain[0])
                V.tensor_tensor(uT[:, 4:6, :], y, cbT[:], ALU.mult).then_inc(conv_ready, 1)
                for t in range(NT):
                    dve.wait_ge(qk_t, 3 + t)
                    V.tensor_copy(kfT[:, :, t * P:(t + 1) * P],
                                  bank[t][0:QK, :].rearrange("p (h s) -> p h s", h=NH)).then_inc(kT_out, 1)
                dve.wait_ge(lam_exp, 1)
                link(V.tensor_tensor(lam[:, 4:5], lam[:, 3:4], lam[:, 2:3], ALU.subtract))
                link(V.tensor_scalar(lam[:, 5:6], const[:, bass.ds(l + K_LI, 1)], -1.0, None, ALU.mult))
                link(V.tensor_tensor(lam[:, 6:7], lam[:, 4:5], lam[:, 5:6], ALU.add))
                link(V.tensor_scalar(lam[:, 7:8], const[:, bass.ds(l + (K_LI + DEPTH), 1)], 1.0, None, ALU.mult))
                link(V.tensor_scalar(cur[:, C_DFG:C_DFG + DV], cur[:, C_DFG:C_DFG + DV], lam[:, 7:8], None, ALU.mult))
                ada_rest(26, ADA_TILES - ADA_FIRST)
                with dve.If(l < 1):
                    dve.drain().then_inc(acc_rest, 1)

                def latent_y():
                    dve.wait_ge(p_act, NH)
                    link(V.reciprocal(ssum[:, 0:NH, :], ssum[:, 0:NH, :]))
                    dve.wait_ge(pv_done, NH)
                    for t in range(NT):
                        ins = V.tensor_tensor(yN[:, t, 0:GW].rearrange("p (h d) -> p h d", h=NH),
                                              bank[6][:, t * GW:(t + 1) * GW].rearrange("p (h d) -> p h d", h=NH),
                                              pair_rows(ssum[:, 0:NH, t], DV), ALU.mult)
                    ins.then_inc(y_ready, 1)

                def diff_y():
                    r = ssum[:, 4:12, :]
                    dve.wait_ge(p_act, 12)
                    link(V.reciprocal(r, r))
                    odd = r.rearrange("p (h two) t -> p h two t", two=2)[:, :, 1, :]
                    link(V.tensor_scalar(odd, odd, lam[:, 6:7], None, ALU.mult))
                    dve.wait_ge(pv_done, 12)
                    o = [tmp[:, t * 512:(t + 1) * 512].rearrange("p (m d) -> p m d", m=8) for t in range(NT)]
                    for t in range(NT):
                        V.tensor_tensor(o[t], bank[7 - t][:, :].rearrange("p (m d) -> p m d", m=8),
                                        pair_rows(ssum[:, 4:12, t], DV), ALU.mult).then_inc(o_read, 1)
                    dve.wait_ge(o_read, 2)
                    od = tmp[:, 1024:1536].rearrange("p (g d) -> p g d", g=NT * NH)
                    for t in range(NT):
                        om = o[t].rearrange("p (h two) d -> p h two d", two=2)
                        link(V.tensor_tensor(od[:, t * NH:(t + 1) * NH, :], om[:, :, 0, :], om[:, :, 1, :], ALU.add))
                    sq = tmp[:, 1536:2048].rearrange("p (g d) -> p g d", g=NT * NH)
                    link(V.tensor_tensor(sq, od, od, ALU.mult))
                    link(V.tensor_reduce(rt[:, 0:8], sq, AX.X, ALU.add))
                    V.tensor_scalar(var[:, 0:8], rt[:, 0:8], 1.0 / DV, RMS_EPS, ALU.mult, ALU.add).then_inc(var_ready, 1)
                    dve.wait_ge(rstd_ready, 2)
                    link(V.tensor_tensor(od, od, pair_rows(rstd[:, 0:8], DV), ALU.mult))
                    V.tensor_tensor(yN[:, :, 512:768].rearrange("p t (h d) -> p t h d", h=NH),
                                    od.rearrange("p (t h) d -> p t h d", t=NT),
                                    cur[:, C_DFG:C_DFG + DV].unsqueeze(1).unsqueeze(1).to_broadcast([P, NT, NH, DV]),
                                    ALU.mult).then_inc(y_ready, 1)

                def mlstm_y():
                    link(V.tensor_scalar(rden[:], den[:], -1.0, None, ALU.mult))
                    link(V.tensor_tensor(rden[:], rden[:], den[:], ALU.max))
                    link(V.tensor_tensor(rden[:], rden[:], nr_em[:, 1, :, :], ALU.max))
                    link(V.reciprocal(rden[:], rden[:]))
                    dve.wait_ge(pv_done, NMAP)
                    for t in range(NT):
                        ins = V.tensor_tensor(t1[:, t * GW:(t + 1) * GW].rearrange("p (h d) -> p h d", h=NH),
                                              bank[7][:, t * GW:(t + 1) * GW].rearrange("p (h d) -> p h d", h=NH),
                                              pair_rows(rden[:, t, :], DV), ALU.mult)
                    link(ins)
                    V.tensor_tensor(yN[:, :, 256:512], t1[:, 0:512].rearrange("p (t n) -> p t n", t=NT), sig_o[:],
                                    ALU.mult).then_inc(y_ready, 1)

                for m in range(NMAP + 2):
                    if m < 12:
                        dve.wait_ge(s_done, m + 1)
                        V.tensor_reduce(nmax[:, m, 0:1], bank[m % 4][:, 0:P], AX.X, ALU.max, negate=True)
                        V.tensor_reduce(nmax[:, m, 1:2], bank[m % 4][:, P:384], AX.X, ALU.max, negate=True).then_inc(max_ready, 1)
                        if m == 2:
                            dve.wait_ge(cols2, 1)
                            mod_columns(1, 3)
                    elif m < NMAP:
                        h = m - 12
                        dve.wait_ge(s_done, m + 1)
                        dve.wait_ge(decay_ready, h + 1)
                        dve.wait_ge(pt_done, m - 2)
                        for t, (lo, hi) in enumerate(((0, P), (P, 384))):
                            ins = V.tensor_tensor_reduce(out=prob[:, m % 3, lo:hi], in0=bank[2 * (h % 2) + 1][:, lo:hi],
                                                         in1=decay[:, h % 2, lo:hi], scale=1.0, scalar=0.0, op0=ALU.mult,
                                                         op1=ALU.add, accum_out=den[:, t, h:h + 1])
                        ins.then_inc(p_dve, 1)
                    if m >= 2:
                        w = m - 2
                        dve.wait_ge(pt_done, w + 1)
                        if w >= 2:
                            dve.wait_ge(pv_done, w - 1)
                        V.tensor_copy(probT[:, w % 2, :], bank[4 + w % 2][:, 0:384]).then_inc(pt_out, 1)
                    if m == NH + 2:
                        latent_y()
                    if m == 12 + 2:
                        diff_y()
                dve.wait_ge(p_dve, NH)
                mlstm_y()

                def next_ada(k, half):
                    base = (l + 1) * ADA_TILES + 6 * k
                    for m in range(3 * half, 3 * half + 3):
                        dve.wait_ge(ada_free, base + (ADA_SLOTS + m - 5))
                        ada_step(m % ADA_SLOTS, (l + 1) * (ADA_TILES // ADA_SLOTS) + 2 * k + half + 1,
                                 c_col[:, k:k + 1] if isinstance(k, int) else c_col[:, bass.ds(k, 1)], m)

                with dve.If(l < DEPTH - 1):
                    dve.wait_ge(acc_bias, 16 * (l + 2))
                    nc.vector.sem_inc(tick, 1)
                    for b in range(ADA_AHEAD):
                        next_ada(b // 2, b % 2)

                def mix_wait(t, half):
                    dve.wait_ge(mix_done, 4 * t + 2 * half + 2)

                for t in range(NT):
                    link(post_norm(t, 0, mix_wait, 3 + 2 * t, lambda: dve.wait_ge(ln_in, 64 * l + 32)))
                    for half in range(2):
                        statistics(t, half)
                    variance(t)
                    dve.wait_ge(rstd_ready, 4 + 2 * t)
                    normalise(t).then_inc(xn_ready, 1)
                    if t == NT - 1:
                        nc.vector.sem_inc(ln1_used, 1)
                evict_x(4, 1, 1)

                sel = rt[:, 0:32]
                selt = sel.rearrange("p (t e) -> p t e", t=NT)
                selg = sel.rearrange("p (g e) -> p g e", e=4)
                pair = rt[:, 32:80].rearrange("p (g e) -> p g e", e=6)
                gs, gm, ge = rt[:, 80:88], rt[:, 88:90], rt[:, 90:98]
                gst, get = gs.rearrange("p (t g) -> p t g", t=NT), ge.rearrange("p (t g) -> p t g", t=NT)
                ms = rt[:, 98:130]
                one = [rt[:, 130:162], rt[:, 162:194]]
                mx, q1 = rt[:, 194:196], rt[:, 196:198]
                ws, wsum = rt[:, 198:230], rt[:, 230:232]
                grp, earlier, rank, most = rt[:, 232:240], rt[:, 240:248], rt[:, 248:250], rt[:, 250:251]
                prio_g = const[:, K_PRIO + N_EXP - N_GRP:K_PRIO + N_EXP].unsqueeze(1).to_broadcast([P, NT, N_GRP])
                prio_e = const[:, K_PRIO:K_PRIO + N_EXP].unsqueeze(1).to_broadcast([P, NT, N_EXP])

                def te(ap):
                    return ap.rearrange("p (t e) -> p t e", t=NT)

                dve.wait_ge(score_ready, 1)
                link(V.tensor_tensor(selt, score[:], b_rt[:].unsqueeze(1).to_broadcast([P, NT, N_EXP]), ALU.add))
                V.tensor_tensor(pair[:, :, 0:3], selg[:, :, 0:3], selg[:, :, 1:4], ALU.add)
                V.tensor_tensor(pair[:, :, 3:5], selg[:, :, 0:2], selg[:, :, 2:4], ALU.add)
                link(V.tensor_tensor(pair[:, :, 5:6], selg[:, :, 0:1], selg[:, :, 3:4], ALU.add))
                link(V.tensor_reduce(gs, pair, AX.X, ALU.max))
                link(V.tensor_reduce(gm, gst, AX.X, ALU.max))
                link(V.tensor_tensor(get, gst, pair_rows(gm, N_GRP), ALU.is_equal))
                link(V.tensor_tensor(get, get, prio_g, ALU.mult))
                link(V.tensor_reduce(gm, get, AX.X, ALU.max))
                link(V.tensor_tensor(get, get, pair_rows(gm, N_GRP), ALU.is_equal))
                V.tensor_copy(group_bf[:], get).then_inc(group_ready, 1)
                link(V.tensor_copy(grp, ge))
                link(V.tensor_scalar(ge, ge, -NEG, NEG, ALU.mult, ALU.add))

                dve.wait_ge(ranks, 1)
                link(V.tensor_reduce(most, bank[0][:, COUNTS + 8:COUNTS + 12], AX.X, ALU.max))
                link(V.tensor_tensor(earlier, bank[0][:, COUNTS:COUNTS + 8], grp, ALU.mult))
                V.tensor_scalar(path[0:1, 0:1], most[0:1, :], float(CAP), None, ALU.is_gt).then_inc(path_ready, 1)
                link(V.tensor_reduce(rank, earlier.rearrange("p (t g) -> p t g", t=NT), AX.X, ALU.add))
                def choose_experts():
                    link(V.tensor_tensor(ms.rearrange("p (g e) -> p g e", e=4), selg, pair_rows(ge, 4), ALU.add))
                    for r in range(2):
                        link(V.tensor_reduce(mx, te(ms), AX.X, ALU.max))
                        link(V.tensor_tensor(te(one[r]), te(ms), pair_rows(mx, N_EXP), ALU.is_equal))
                        link(V.tensor_tensor(te(one[r]), te(one[r]), prio_e, ALU.mult))
                        link(V.tensor_reduce(q1, te(one[r]), AX.X, ALU.max))
                        link(V.tensor_tensor(te(one[r]), te(one[r]), pair_rows(q1, N_EXP), ALU.is_equal))
                        if r == 0:
                            link(V.scalar_tensor_tensor(out=ms, in0=one[0], scalar=NEG, in1=ms, op0=ALU.mult, op1=ALU.add))
                    link(V.tensor_tensor(one[0], one[0], one[1], ALU.add))
                    link(V.tensor_tensor(te(ws), score[:], te(one[0]), ALU.mult))
                    link(V.tensor_reduce(wsum, te(ws), AX.X, ALU.add))
                    link(V.reciprocal(wsum, wsum))
                    link(V.tensor_tensor(gates[:], te(ws), pair_rows(wsum, N_EXP), ALU.mult))

                def ada_while_sorting():
                    with dve.If(l < DEPTH - 1):
                        for b in range(ADA_AHEAD, 2 * ADA_AHEAD):
                            next_ada(b // 2, b % 2)

                nc.vector.sem_inc(h_ready, 2)
                dve.wait_ge(path_ready, 1)
                crowded = nc.values_load(path[0:1, 0:1], engines=[ENG.DVE], min_val=0, max_val=1)
                links = chain[0]
                with dve.If(crowded < 1):
                    for t in range(NT):
                        for g in range(N_GRP):
                            ins = V.tensor_scalar(to_slot[:, t, g * CAP:(g + 1) * CAP], const[:, K_IOTA:K_IOTA + CAP],
                                                  rank[:, t:t + 1], grp[:, t * N_GRP + g:t * N_GRP + g + 1],
                                                  ALU.is_equal, ALU.mult)
                    ins.then_inc(to_slot_ready, 1)
                    choose_experts()

                    def gate_move(g, j):
                        for t in range(NT):
                            ins = V.tensor_scalar(gmove[:, j % 2, t * CAP:(t + 1) * CAP],
                                                  to_slot[:, t, g * CAP:(g + 1) * CAP] if isinstance(g, int) else
                                                  to_slot[:, t, bass.ds(g * CAP, CAP)],
                                                  gates[:, t, bass.ds(4 * g + j, 1)], None, ALU.mult)
                        ins.then_inc(diag_ready, 1)

                    def hidden(g, j):
                        done = 4 * g + j + 1
                        dve.wait_ge(silu_done, done)
                        dve.wait_ge(g_ready, done)
                        gate = bank[2][:, (j % 2) * CAP:(j % 2 + 1) * CAP].unsqueeze(1).to_broadcast([P, 2, CAP])
                        V.tensor_tensor(sgate[:, j % 2, :].rearrange("p (c n) -> p c n", c=2),
                                        silu[:, j % 2, :].rearrange("p (c n) -> p c n", c=2), gate,
                                        ALU.mult).then_inc(sg_done, 1)
                        dve.wait_ge(sg_done, done)
                        dve.wait_ge(h_done, done)
                        V.tensor_tensor(hT[:, j % 2, :], sgate[:, j % 2, :], bank[j % 2][:, S:2 * S],
                                        ALU.mult).then_inc(h_ready, 1)

                    def group_out(g):
                        dve.wait_ge(yg_done, g + 2)
                        V.tensor_copy(yg[:, g, 512:1024], bank[5][:, :]).then_inc(yg_dve, 1)

                    dve.wait_ge(to_slot_ready, 1)
                    for j in range(2):
                        gate_move(0, j)
                    nc.vector.sem_inc(yg_dve, 1)
                    ada_while_sorting()
                    dve.wait_ge(turned_back, 2)
                    V.tensor_copy(from_slot[:, 1, :], bank[7][:, :]).then_inc(from_dve, 1)
                    def group(g, with_ada):
                        for j in range(4):
                            hidden(g, j)
                            if j < 2:
                                gate_move(g, j + 2)
                            else:
                                gate_move(g + 1, j - 2)
                            if with_ada:
                                with dve.If(l < DEPTH - 1):
                                    next_ada(2 * g + (ADA_AHEAD + j // 2), j % 2)
                        group_out(g)

                    with dve.Fori(0, ADA_LATE // 4) as g:
                        group(g, True)
                    with dve.Fori(ADA_LATE // 4, N_GRP - 1) as g:
                        group(g, False)
                    for j in range(4):
                        hidden(N_GRP - 1, j)
                        if j < 2:
                            gate_move(N_GRP - 1, j + 2)
                    group_out(N_GRP - 1)
                with dve.If(crowded > 0):
                    chain[0] = links
                    choose_experts()

                    def expert(i, j):
                        for t in range(NT):
                            ins = V.tensor_scalar(gmove[:, j, t * P:(t + 1) * P], ident, gates[:, t, bass.ds(2 * i + j, 1)],
                                                  None, ALU.mult)
                        ins.then_inc(diag_ready, 1)
                        for c in range(2):
                            s = 2 * j + c
                            dve.wait_ge(silu_done, 4 * i + s + 1)
                            if c == 0:
                                dve.wait_ge(g_ready, 2 * i + j + 1)
                            V.tensor_tensor(sgate[:, c, :], silu[:, c, :], bank[6 + j][:, 0:S], ALU.mult).then_inc(sg_done, 1)
                            dve.wait_ge(sg_done, 4 * i + s + 1)
                            dve.wait_ge(y_step, 4 * i + s + 1)
                            V.tensor_tensor(hT[:, c, :], sgate[:, c, :], bank[4 + c][:, S:2 * S], ALU.mult).then_inc(h_ready, 1)

                    ada_while_sorting()
                    with dve.Fori(0, ADA_LATE // 2) as i:
                        for j in range(2):
                            expert(i, j)
                            with dve.If(l < DEPTH - 1):
                                next_ada(i + ADA_AHEAD, j)
                    with dve.Fori(ADA_LATE // 2, N_EXP // 2) as i:
                        for j in range(2):
                            expert(i, j)
                for t in range(NT):
                    post_norm(t, 1, lambda t, half: dve.wait_ge(moe_done, 2 * t + half + 1), 7 + t,
                              lambda: dve.wait_ge(ln_in, 64 * l + 64)).then_inc(x_done, 1)
                    with dve.If(l < DEPTH - 1):
                        dve.wait_ge(x_done, t + 1)
                        entry_variance(t, 3 * NT * (l + 1) + 3 * t)
                        dve.wait_ge(entry_rstd, NT * (l + 1) + (t + 1))
                        normalise(t).then_inc(entry_ready, 1)
                end_of_layer(dve, l)

        @block.tensor
        def _(pe):
            nc.tensor.sem_inc(w_free, W_SLOTS)
            nc.tensor.sem_inc(up_free, 2)
            nc.tensor.sem_inc(down_free, 2)
            pe.wait_ge(setup, 4)
            pe.wait_ge(im_ready, 2)
            pe.wait_ge(ident_in, 16)

            owed = []

            def then_free(mm):
                if owed:
                    mm.then_inc(owed.pop(), 1)
                return mm

            def mod_col(b, section, j):
                for k in range(KC):
                    cols = mod_acc[:, section * D + k:section * D + k + KC * (P - 1) + 1:KC]
                    c0 = (j * KC + k) * MOD_W
                    mm = pe.matmul(bank[b][:, c0:c0 + MOD_W], cols, ones[:, 0:MOD_W], start=True, stop=True)
                return mm

            def turn_x(first_bank, t):
                for k in range(KC):
                    c0 = (k % 4) * P
                    pe.transpose(bank[first_bank + 2 * t + k // 4][:, c0:c0 + P], xn[:, t, k:k + KC * (P - 1) + 1:KC],
                                 ident).then_inc(xt_done, 1)

            def w_step(l, n, half):
                kind, width = W_IN_TILES[n][2], W_IN_TILES[n][1]
                step = 2 * n + half
                w = w_ring[n % W_SLOTS]
                dst = bank[4 + step % 4]
                hi, lo = w_hi[n % W_HI], w_lo[n % W_SLOTS]
                if half == 0:
                    pe.wait_ge(hi_ready, n + 1)
                    pe.wait_ge(lo_ready, n + 1)
                if step >= 4:
                    pe.wait_ge(z_out, step - 3)
                if step < 2:
                    pe.wait_ge(u_split, step + 1)
                turned = kind in ("mq", "mk", "cb", "cc", "ch")
                for k in range(KC):
                    for q, (u, wt) in enumerate(((u_hi, hi), (u_hi, lo), (u_lo, hi))):
                        first, final = k == 0 and q == 0, k == KC - 1 and q == 2
                        if turned:
                            mm = pe.matmul(dst[:, 0:S], wt[:, k, half * P:(half + 1) * P], u[:, k, :], start=first, stop=final)
                        else:
                            mm = pe.matmul(dst[:, 0:width], u[:, k, half * P:(half + 1) * P], wt[:, k, 0:width],
                                           start=first, stop=final)
                        if first:
                            then_free(mm)
                mm.then_inc(z_done, 1)
                if half == 1:
                    owed.append(w_free)

            def turn_latents():
                pe.wait_ge(lat_ready, 1)
                for t in range(NT):
                    then_free(pe.transpose(bank[0][:, t * P:(t + 1) * P], zA[:, t, 0:P], ident))
                    mm = pe.transpose(bank[0][:, S + t * P:S + (t + 1) * P], zA[:, t, Q_LORA:Q_LORA + KV_LORA], ident)
                mm.then_inc(lat_t, 1)
                for t in range(NT):
                    mm = pe.transpose(bank[1][0:Q_LORA - P, t * P:(t + 1) * P], zA[:, t, P:Q_LORA], ident)
                mm.then_inc(lat_t, 1)

            def turn_gates():
                pe.wait_ge(z_out, 12)
                for q in range(2):
                    for t in range(NT):
                        mm = pe.transpose(bank[2][0:NH, q * S + t * P:q * S + (t + 1) * P], zG[:, t, q * NH:(q + 1) * NH], ident)
                mm.then_inc(gate_t, 1)

            def project_latents():
                pe.wait_ge(lat_act, 1)
                pe.wait_ge(lat_dve, 1)
                for t in range(NT):
                    dst = bank[3 if t == 0 else 1][:, 0:NH * QK]
                    then_free(pe.matmul(dst, pT0[:, t * P:(t + 1) * P], uq[:], start=True, stop=False))
                    pe.matmul(dst, pT1[:, t * P:(t + 1) * P], uq_b[:], start=False, stop=True).then_inc(proj_done, 1)
                for t in range(NT):
                    if t == 1:
                        pe.wait_ge(rows_ready, 1)
                    pe.matmul(bank[0 if t == 0 else 2][:, :], pT0[:, S + t * P:S + (t + 1) * P], ukv[:], start=True,
                              stop=True).then_inc(proj_done, 1)

            def turn_diff():
                pe.wait_ge(d_roped, 1)
                for t in range(NT):
                    if t == 0:
                        pe.wait_ge(kv_out, 1)
                    else:
                        pe.wait_ge(q_out, 2)
                    for b in range(4):
                        if b == 1:
                            then_free(mm)
                        mm = pe.transpose(bank[t][:, b * P:(b + 1) * P], zD[:, t, b * P:(b + 1) * P], ident)
                    mm.then_inc(d_t, 1)

            def turn_rows():
                pe.wait_ge(q_out, 1)
                for q, row in enumerate((3, 2)):
                    for t in range(NT):
                        mm = pe.transpose(bank[3][:, q * 8 + t * NH:q * 8 + (t + 1) * NH], rows[:, row, t * P:(t + 1) * P],
                                          ident[0:NH, 0:NH])
                mm.then_inc(rows_t, 1)

            def turn_qk():
                pe.wait_ge(qk_ready, 1)
                pe.wait_ge(kv_out, 2)
                pe.wait_ge(rows_out, 1)
                pe.wait_ge(d_out, 2)
                for q, src in enumerate((qf, kf)):
                    for t in range(NT):
                        dst = bank[2 + t if q == 0 else t]
                        for h in range(NH):
                            mm = pe.transpose(dst[0:QK, h * P:(h + 1) * P], src[:, t, h * QK:(h + 1) * QK], ident)
                        mm.then_inc(qk_t, 1)

            def gate_rows():
                pe.wait_ge(acc_rest, 1)
                for g, section in enumerate((2, 5)):
                    for half in range(2):
                        pe.wait_ge(z_out, 24)
                        c0 = section * D + half * 512
                        pe.matmul(bank[4 + 2 * g + half][:, :], ones[:], mod_acc[:, c0:c0 + 512], start=True,
                                  stop=True).then_inc(rows_g, 1)

            def columns_2():
                pe.wait_ge(acc_rest, 1)
                pe.wait_ge(qT_out, 2)
                mod_col(3, 3, 0)
                mod_col(3, 4, 1).then_inc(cols2, 1)

            def scores(m):
                if m < 4:
                    q, k = qfT[:, m, :], kfT[:, m, :]
                    dst = bank[m % 4]
                    if m == 0:
                        pe.wait_ge(qT_out, 2)
                        pe.wait_ge(kT_out, 2)
                    if m == 3:
                        pe.wait_ge(mcol_ready, 2)
                elif m < 12:
                    j = m - 4
                    r = slice(DK * (j % 4), DK * (j % 4) + DK)
                    q, k = dT[r, j // 4, :], dT[r, 2 + j // 4, :]
                    dst = bank[j % 4]
                    pe.wait_ge(p_act, m - 3)
                else:
                    h = m - 12
                    r = slice(DV * (h % 2), DV * (h % 2) + DV)
                    q, k = mqT[r, h // 2, :], mkT[r, h // 2, :]
                    dst = bank[2 * (h % 2) + 1]
                    if h < 2:
                        pe.wait_ge(p_act, 10 + 2 * h)
                    else:
                        pe.wait_ge(p_dve, h - 1)
                    log_decay = bank[2 * (h % 2)]
                    sel = head_sel[:, h * P:(h + 1) * P]
                    pe.matmul(log_decay[:, 0:P], sel, rows[:, 1, 0:P], start=True, stop=False)
                    pe.matmul(log_decay[:, 0:P], ident_bf, mask_bf, start=False, stop=True)
                    pe.matmul(log_decay[:, P:384], sel, rows[:, 1, :], start=True, stop=False)
                    pe.matmul(log_decay[:, 256:384], ident_bf, mask_bf, start=False, stop=True)
                    pe.matmul(dst[:, 0:P], q[:, 0:P], k[:, 0:P], start=True, stop=True)
                    return pe.matmul(dst[:, P:384], q[:, P:S], k, start=True, stop=True)
                pe.matmul(dst[:, 0:P], q[:, 0:P], k[:, 0:P], start=True, stop=False)
                pe.matmul(dst[:, 0:P], ident_bf, mask_bf, start=False, stop=True)
                pe.matmul(dst[:, P:384], q[:, P:S], k, start=True, stop=False)
                return pe.matmul(dst[:, 256:384], ident_bf, mask_bf, start=False, stop=True)

            def turn_probs(m):
                pe.wait_ge(p_act if m < 12 else p_dve, m + 1 if m < 12 else m - 11)
                if m >= 2:
                    pe.wait_ge(pt_out, m - 1)
                if m < 2:
                    pe.wait_ge(rows_g_out, 2)
                for b in range(3):
                    mm = pe.transpose(bank[4 + m % 2][:, b * P:(b + 1) * P], prob[:, m % 3, b * P:(b + 1) * P], ident)
                mm.then_inc(pt_done, 1)

            def values(m):
                pe.wait_ge(pt_out, m + 1)
                pT = probT[:, m % 2, :]
                if m < 4:
                    v_ = [kvn[:, t, m * 2 * DV + DV:(m + 1) * 2 * DV] for t in range(NT)]
                    dst = [bank[6][:, t * GW + m * DV:t * GW + (m + 1) * DV] for t in range(NT)]
                    if m == 0:
                        pe.wait_ge(rows_g_out, 4)
                elif m < 12:
                    j = m - 4
                    v_ = [zD[:, t, 512 + (j // 2) * DV:512 + (j // 2 + 1) * DV] for t in range(NT)]
                    dst = [bank[7 - t][:, j * DV:(j + 1) * DV] for t in range(NT)]
                    if m == 4:
                        pe.wait_ge(y_ready, 1)
                else:
                    h = m - 12
                    v_ = [m_v[:, t, h * DV:(h + 1) * DV] for t in range(NT)]
                    dst = [bank[7][:, t * GW + h * DV:t * GW + (h + 1) * DV] for t in range(NT)]
                    if h == 0:
                        pe.wait_ge(o_read, 2)
                pe.matmul(dst[0], pT[:, 0:P], v_[0], start=True, stop=True)
                pe.matmul(dst[1], pT[:, P:S], v_[0], start=True, stop=False)
                pe.matmul(dst[1], pT[:, S:384], v_[1], start=False, stop=True).then_inc(pv_done, 1)

            def turn_y(n):
                c0 = (0, 512, 256)[n]
                pe.wait_ge(y_ready, n + 1)
                if n == 0:
                    pe.wait_ge(pt_out, NMAP)
                for c in range(2):
                    for t in range(NT):
                        mm = pe.transpose(bank[4 + n][:, c * S + t * P:c * S + (t + 1) * P],
                                          yN[:, t, c0 + c * P:c0 + (c + 1) * P], ident)
                mm.then_inc(y_t, 1)

            def w_out_step(l, t, s):
                n = NW_IN + s
                w = w_ring[n % W_SLOTS]
                if t == 0:
                    pe.wait_ge(w_in_sem[n % W_SLOTS], 16 * (l * (W_TILES // W_SLOTS) + n // W_SLOTS + 1))
                if t == 0 and s == 0:
                    pe.wait_ge(conv_ready, 1)
                    pe.wait_ge(y_out_act, 3)
                    pe.wait_ge(p_act, 12)
                    pe.wait_ge(p_dve, NH)
                for k in range(KC):
                    mm = pe.matmul(bank[2 * t + s // 2][:, (s % 2) * 256:(s % 2 + 1) * 256], uT[:, k, t * P:(t + 1) * P],
                                   w[:, k, 0:256], start=(k == 0), stop=(k == KC - 1))
                    if k == 0:
                        then_free(mm)
                mm.then_inc(mix_done, 1)
                if t == NT - 1:
                    owed.append(w_free)

            def router(t):
                for k in range(KC):
                    if t == 0:
                        pe.wait_ge(ut_act, KC + k + 1)
                    elif k == 0:
                        pe.wait_ge(ut_act, 2 * KC + KC // 2)
                        pe.wait_ge(ut_dve, KC + KC // 2)
                    mm = pe.matmul(bank[0][:, t * N_EXP:(t + 1) * N_EXP], uT[:, k, t * P:(t + 1) * P], w_rt[:, k, :],
                                   start=(k == 0), stop=(k == KC - 1))
                    if k == 0:
                        then_free(mm)
                return mm

            def expert_up(l, i, s):
                j, c = s // 2, s % 2
                if c == 0:
                    for q in range(2):
                        pe.wait_ge(e_in_sem[3 * j + q], 16 * (l * (N_EXP // 2) + i + 1))
                pe.wait_ge(h_ready, 4 * i + s + 1)
                for q in range(2):
                    w = e_ring[3 * j + q][:].rearrange("p (k f) -> p k f", k=KC)
                    for k in range(KC):
                        mm = pe.matmul(bank[4 + c][:, q * S:(q + 1) * S], w[:, k, c * P:(c + 1) * P], uT[:, k, :],
                                       start=(k == 0), stop=(k == KC - 1))
                        if q == 0 and k == 0:
                            mm.then_inc(y_step, 1)
                mm.then_inc(h_done, 1)

            def expert_gate(i, j):
                pe.wait_ge(diag_ready, 2 * i + j + 1)
                pe.matmul(bank[6 + j][:, 0:S], ones[:], gmove[:, j, :], start=True, stop=True).then_inc(g_ready, 1)

            def expert_down(l, i, s):
                j, c = s // 2, s % 2
                if c == 0:
                    pe.wait_ge(e_in_sem[3 * j + 2], 16 * (l * (N_EXP // 2) + i + 1))
                pe.wait_ge(h_ready, 4 * i + s + 3)
                w = e_ring[3 * j + 2][:].rearrange("p (c n) -> p c n", c=2)
                for t in range(NT):
                    for half in range(2):
                        mm = pe.matmul(bank[2 * t + half][:, :], hT[:, c, t * P:(t + 1) * P],
                                       w[:, c, half * 512:(half + 1) * 512], start=False, stop=False, skip_group_check=True)
                        if c == 0 and t == 0 and half == 0:
                            mm.then_inc(up_free, 1)
                if c == 1:
                    mm.then_inc(down_free, 1)

            def keep_warm(dst, n):
                for _ in range(n):
                    pe.matmul(dst, zeros_bf[:, 0:P], zeros_bf[:, 0:dst.shape[1]], start=True, stop=True)

            def bracket(start):
                for b in range(4):
                    mm = pe.matmul(bank[b][:, :], zeros_bf[:, 0:P], zeros_bf[:], start=start, stop=not start,
                                   skip_group_check=True)
                    if not start:
                        mm.then_inc(moe_done, 1)

            def count_tokens():
                pe.wait_ge(group_ready, 1)
                pe.matmul(bank[0][:, COUNTS + 0:COUNTS + 4], before_bf[:], group_bf[:, 0, :], start=True, stop=True)
                pe.matmul(bank[0][:, COUNTS + 4:COUNTS + 8], before_bf[:], group_bf[:, 1, :], start=True, stop=False)
                pe.matmul(bank[0][:, COUNTS + 4:COUNTS + 8], ones_bf[:], group_bf[:, 0, :], start=False, stop=True)
                pe.matmul(bank[0][:, COUNTS + 8:COUNTS + 12], ones_bf[:], group_bf[:, 0, :], start=True, stop=False)
                pe.matmul(bank[0][:, COUNTS + 8:COUNTS + 12], ones_bf[:], group_bf[:, 1, :], start=False, stop=True).then_inc(ranks, 1)

            def sort_tokens():
                pe.wait_ge(to_slot_ready, 1)
                for k in range(KC):
                    for t in range(NT):
                        mm = pe.matmul(bank[k][:, :], xn[:, t, k:k + KC * (P - 1) + 1:KC], to_slot[:, t, :],
                                       start=(t == 0), stop=(t == NT - 1))
                    mm.then_inc(sorted_done, 1)

            def group_up(l, g, j, first=False):
                for q in range(2):
                    pe.wait_ge(e_in_sem[3 * (j % 2) + q], 16 * (l * (N_EXP // 2) + 2 * g + j // 2 + 1))
                pe.wait_ge(h_ready, 4 * g + j + 1)
                for q in range(2):
                    w = e_ring[3 * (j % 2) + q][:].rearrange("p (k f) -> p k f", k=KC)
                    for c in range(2):
                        for k in range(KC):
                            if first and q == 0 and c == 0:
                                pe.wait_ge(us_act, k + 1)
                            moving = uTs[:, k, g * CAP:(g + 1) * CAP] if isinstance(g, int) else uTs[:, k, bass.ds(g * CAP, CAP)]
                            mm = pe.matmul(bank[j % 2][:, (2 * q + c) * CAP:(2 * q + c + 1) * CAP],
                                           w[:, k, c * P:(c + 1) * P], moving, start=(k == 0), stop=(k == KC - 1))
                            if q == 0 and c == 0 and k == 0 and not first:
                                mm.then_inc(up_free, 1)
                mm.then_inc(h_done, 1)

            def turn_back():
                for t in range(NT):
                    for g in range(N_GRP):
                        mm = pe.transpose(bank[6 + t][:, g * CAP:(g + 1) * CAP], to_slot[:, t, g * CAP:(g + 1) * CAP], ident)
                    mm.then_inc(turned_back, 1)

            def group_gate(g, j):
                pe.wait_ge(diag_ready, 4 * g + j + 1)
                for t in range(NT):
                    mm = pe.matmul(bank[2][:, (j % 2) * CAP:(j % 2 + 1) * CAP], ones[:], gmove[:, j % 2, t * CAP:(t + 1) * CAP],
                                   start=(t == 0), stop=(t == NT - 1))
                    if t == 0 and j == 0:
                        mm.then_inc(yg_done, 1)
                mm.then_inc(g_ready, 1)

            def group_down(l, g, j, last=False):
                pe.wait_ge(e_in_sem[3 * (j % 2) + 2], 16 * (l * (N_EXP // 2) + 2 * g + j // 2 + 1))
                pe.wait_ge(h_ready, 4 * g + j + 3)
                if j == 0:
                    pe.wait_ge(yg_act, g + 1)
                    pe.wait_ge(yg_dve, g + 1)
                w = e_ring[3 * (j % 2) + 2][:].rearrange("p (c n) -> p c n", c=2)
                for half in range(2):
                    for c in range(2):
                        mm = pe.matmul(bank[4 + half][:, :], hT[:, j % 2, c * CAP:(c + 1) * CAP],
                                       w[:, c, half * 512:(half + 1) * 512], start=(j == 0 and c == 0),
                                       stop=(j == 3 and c == 1))
                        if last and half == 0 and c == 0:
                            mm.then_inc(up_free, 1)
                mm.then_inc(yg_done if last else down_free, 1)

            def scatter():
                pe.wait_ge(from_act, 1)
                pe.wait_ge(from_dve, 1)
                pe.wait_ge(yg_act, N_GRP)
                pe.wait_ge(yg_dve, N_GRP)

                def put(t, half, g):
                    return pe.matmul(bank[2 * t + half][:, :], from_slot[:, t, g * CAP:(g + 1) * CAP],
                                     yg[:, g, half * 512:(half + 1) * 512], start=(g == 0), stop=(g == N_GRP - 1))

                for t in range(NT):
                    for half in range(2):
                        for g in range(N_GRP - 1):
                            mm = put(t, half, g)
                            if t == 0 and half == 0 and g == 0:
                                mm.then_inc(down_free, 1)
                        if t == 0:
                            pe.wait_ge((yg_act, yg_dve)[half], N_GRP + 1)
                        put(t, half, N_GRP - 1).then_inc(moe_done, 1)

            with pe.Fori(0, DEPTH) as l:
                for t in range(NT):
                    pe.wait_ge(entry_ready, NT * l + (t + 1))
                    turn_x(0, t)
                pe.wait_ge(acc_first, 1)
                mod_col(7, 0, 0)
                mod_col(7, 1, 1).then_inc(mod_cols, 1)
                for n in range(NW_IN):
                    for half in range(2):
                        if n == 1 and half == 1:
                            pe.wait_ge(mcol_ready, 1)
                        w_step(l, n, half)
                    if n == 7:
                        turn_latents()
                        turn_gates()
                    if n == 9:
                        project_latents()
                    if n == 11:
                        turn_diff()
                        turn_rows()
                pe.wait_ge(z_out, 21)
                turn_qk()
                keep_warm(bank[4][:, :], 10)
                with pe.If(l > 0):
                    gate_rows()
                for m in range(NMAP + 3):
                    if m < NMAP:
                        scores(m).then_inc(s_done, 1)
                    if m == 2:
                        with pe.If(l < 1):
                            gate_rows()
                        columns_2()
                    if 2 <= m < NMAP + 2:
                        turn_probs(m - 2)
                    if m >= 3:
                        values(m - 3)
                for n in range(3):
                    turn_y(n)
                for t in range(NT):
                    for s in range(W_OUT_TILES):
                        w_out_step(l, t, s)
                for t in range(NT):
                    pe.wait_ge(xn_ready, t + 1)
                    turn_x(4, t)
                    router(t).then_inc(logits, 1)
                count_tokens()
                pe.wait_ge(path_ready, 1)
                crowded = nc.values_load(path[0:1, 0:1], engines=[ENG.PE], min_val=0, max_val=1)
                last = N_EXP // 2 - 1
                with pe.If(crowded < 1):
                    sort_tokens()
                    group_up(l, 0, 0, first=True)
                    turn_back()
                    with pe.Fori(0, N_GRP - 1) as g:
                        for j in range(4):
                            group_gate(g, j)
                            if j < 3:
                                group_up(l, g, j + 1)
                            else:
                                group_up(l, g + 1, 0)
                            group_down(l, g, j)
                    for j in range(4):
                        group_gate(N_GRP - 1, j)
                        if j < 3:
                            group_up(l, N_GRP - 1, j + 1)
                        group_down(l, N_GRP - 1, j, last=(j == 3))
                    scatter()
                with pe.If(crowded > 0):
                    bracket(True)
                    expert_up(l, 0, 0)
                    with pe.Fori(0, last) as i:
                        for s in range(4):
                            if s % 2 == 0:
                                expert_gate(i, s // 2)
                            if s < 3:
                                expert_up(l, i, s + 1)
                            else:
                                expert_up(l, i + 1, 0)
                            expert_down(l, i, s)
                    for s in range(4):
                        if s % 2 == 0:
                            expert_gate(last, s // 2)
                        if s < 3:
                            expert_up(l, last, s + 1)
                        expert_down(l, last, s)
                    bracket(False)
                end_of_layer(pe, l)


_INS = ["x", "c", "w_ada", "b_ada", "w_in", "mla_g_q", "mla_g_kv", "mla_w_uq", "mla_w_ukv", "ml_b_i", "ml_b_f",
        "sc_w", "df_lq1", "df_lk1", "df_lq2", "df_lk2", "df_g", "w_out", "ln1_g", "ln1_b", "w_router", "b_router",
        "w1", "w3", "w2", "ln2_g", "ln2_b"]


def kernel(**inputs):
    import concourse.bacc as _bacc
    from concourse.bass_utils import run_bass_kernel_spmd as _run

    nc = _bacc.Bacc("TRN2", target_bir_lowering=False, num_devices=1, dynamic_dma_scratch_size=1024)
    arrays = {f"in_{name}": np.ascontiguousarray(inputs[name]) for name in _INS}
    arrays["in_const"], arrays["in_ident_mask"], arrays["in_head_sel"] = shape_constants()
    aps = {}
    for name, arr in arrays.items():
        aps[name[3:]] = nc.dram_tensor(name, arr.shape, mybir.dt.from_np(arr.dtype), kind="ExternalInput").ap()
    out = nc.dram_tensor("out_0", (1, S, D), F32, kind="ExternalOutput").ap()
    build(nc, aps, out)
    r = _run(nc, [arrays], core_ids=[0])
    return r.results[0]["out_0"]
```
